# Optimizing a Trainium2 kernel written in Bass

```python
import jax, jax.numpy as jnp
from jax import lax
import numpy as np

D_MODEL = 1024
BATCH = 1
SEQ = 1024
DEPTH = 2

CHUNK = 64
EPS = 1e-6
NEG = -1e30
TINY = 1e-30
N_BRANCH = 3
BR_WIDTH = D_MODEL // 2

A_HEADS = 4
A_DK = BR_WIDTH // A_HEADS
A_DV = BR_WIDTH // A_HEADS

B_HEADS = 8
B_KV_HEADS = 2
B_HD = BR_WIDTH // B_HEADS
B_GROUP = B_HEADS // B_KV_HEADS
B_ROT = B_HD // 4
ROPE_THETA = 500000.0
WINDOW = 128
WIN_PREV_CHUNKS = WINDOW // CHUNK - 1

C_HEADS = 4
C_DK = BR_WIDTH // C_HEADS
C_DV = BR_WIDTH // C_HEADS
CONV_W = 4

SPLIT_SIZES = (
    A_HEADS * A_DK, A_HEADS * A_DK, A_HEADS * A_DV, BR_WIDTH,
    B_HEADS * B_HD, B_KV_HEADS * B_HD, B_KV_HEADS * B_HD, BR_WIDTH,
    2 * C_HEADS * C_DK, C_HEADS * C_DV, 2 * C_HEADS, C_HEADS * C_DV, BR_WIDTH,
)
N_IN = sum(SPLIT_SIZES)

kernel_name = "hybrid_hgrn2_swa_mlstm_gated"

def rms_norm(x, g):
    xf = x.astype(jnp.float32)
    y = xf * lax.rsqrt(jnp.mean(xf * xf, axis=-1, keepdims=True) + EPS)
    return (y * g.astype(jnp.float32)).astype(x.dtype)

def head_rms_norm(t, g, n_heads):
    b, s, w = t.shape
    d = w // n_heads
    tf = t.astype(jnp.float32).reshape(b, s, n_heads, d)
    tf = tf * lax.rsqrt(jnp.mean(tf * tf, axis=-1, keepdims=True) + EPS)
    tf = tf * g.astype(jnp.float32).reshape(-1, d)
    return tf.reshape(b, s, w)

def to_chunks(t, n_heads):
    b, s, w = t.shape
    t = t.reshape(b, s // CHUNK, CHUNK, n_heads, w // n_heads)
    return t.transpose(1, 0, 3, 2, 4)

def from_chunks(t):
    nc, b, h, l, d = t.shape
    return t.transpose(1, 0, 3, 2, 4).reshape(b, nc * l, h * d)

def causal_depthwise_conv(t, w, bias):
    out = lax.conv_general_dilated(
        t, w[:, None, :].astype(t.dtype), window_strides=(1,),
        padding=((CONV_W - 1, 0),), dimension_numbers=('NWC', 'WIO', 'NWC'),
        feature_group_count=t.shape[-1])
    return out + bias.astype(t.dtype)

def partial_rope(t, pos):
    half = B_ROT // 2
    inv_freq = ROPE_THETA ** (-jnp.arange(half, dtype=jnp.float32) / half)
    ang = pos.astype(jnp.float32)[:, None] * inv_freq[None, :]
    cos = jnp.cos(ang)[None, :, None, :]
    sin = jnp.sin(ang)[None, :, None, :]
    tf = t.astype(jnp.float32)
    t1, t2, rest = tf[..., :half], tf[..., half:B_ROT], tf[..., B_ROT:]
    out = jnp.concatenate([t1 * cos - t2 * sin, t2 * cos + t1 * sin, rest], axis=-1)
    return out.astype(t.dtype)

def hgrn2_mixer(q_raw, f_raw, i_raw, lb, norm_g):
    b, s, _ = q_raw.shape
    f32 = jnp.float32
    lbf = lb.astype(f32)
    f = lbf + (1.0 - lbf) * jax.nn.sigmoid(f_raw.astype(f32))
    log_f = jnp.log(jnp.maximum(f, TINY))
    k = 1.0 - f
    q = jax.nn.silu(q_raw.astype(f32)) * (A_DK ** -0.5)
    v = i_raw.astype(f32)
    qc, kc, gc = to_chunks(q, A_HEADS), to_chunks(k, A_HEADS), to_chunks(log_f, A_HEADS)
    vc = to_chunks(v, A_HEADS)
    mask = jnp.tril(jnp.ones((CHUNK, CHUNK), dtype=bool))

    def step(state, inp):
        qt, kt, vt, gt = inp
        cum = jnp.cumsum(gt, axis=2)
        diff = cum[:, :, :, None, :] - cum[:, :, None, :, :]
        decay = jnp.exp(jnp.where(mask[:, :, None], diff, NEG))
        scores = jnp.einsum('bhtd,bhtsd,bhsd->bhts', qt, decay, kt)
        out = (jnp.einsum('bhts,bhsv->bhtv', scores, vt)
               + jnp.einsum('bhtd,bhdv->bhtv', qt * jnp.exp(cum), state))
        last = cum[:, :, -1:, :]
        state = (jnp.exp(last[:, :, 0, :])[..., None] * state
                 + jnp.einsum('bhsd,bhsv->bhdv', kt * jnp.exp(last - cum), vt))
        return state, out

    s0 = jnp.zeros((b, A_HEADS, A_DK, A_DV), f32)
    _, o = lax.scan(step, s0, (qc, kc, vc, gc))
    return head_rms_norm(from_chunks(o), norm_g, A_HEADS)

def swa_sink_attention(q, k, v, sinks, pos):
    b, s, _ = q.shape
    nc = s // CHUNK
    q = partial_rope(q.reshape(b, s, B_HEADS, B_HD), pos)
    k = partial_rope(k.reshape(b, s, B_KV_HEADS, B_HD), pos)
    v = v.reshape(b, s, B_KV_HEADS, B_HD)
    q = q.reshape(b, nc, CHUNK, B_KV_HEADS, B_GROUP, B_HD)
    k = k.reshape(b, nc, CHUNK, B_KV_HEADS, B_HD)
    v = v.reshape(b, nc, CHUNK, B_KV_HEADS, B_HD)
    npv = WIN_PREV_CHUNKS
    pad = ((0, 0), (npv, 0), (0, 0), (0, 0), (0, 0))
    kp, vp = jnp.pad(k, pad), jnp.pad(v, pad)
    kb = jnp.concatenate([kp[:, j:j + nc] for j in range(npv + 1)], axis=2)
    vb = jnp.concatenate([vp[:, j:j + nc] for j in range(npv + 1)], axis=2)
    chunk_idx = jnp.arange(nc)[:, None] - npv + jnp.arange(npv + 1)[None, :]
    valid = jnp.repeat(chunk_idx >= 0, CHUNK, axis=1)
    scores = jnp.einsum('bclkgd,bcmkd->bkgclm', q, kb).astype(jnp.float32) * (B_HD ** -0.5)
    scores = jnp.where(valid[None, None, None, :, None, :], scores, NEG)
    sink = sinks.astype(jnp.float32).reshape(1, B_KV_HEADS, B_GROUP, 1, 1, 1)
    mx = jnp.maximum(jnp.max(scores, axis=-1, keepdims=True), sink)
    p = jnp.exp(scores - mx)
    p = p / (jnp.sum(p, axis=-1, keepdims=True) + jnp.exp(sink - mx))
    out = jnp.einsum('bkgclm,bcmkd->bclkgd', p.astype(vb.dtype), vb)
    return out.reshape(b, s, B_HEADS * B_HD)

def mlstm_mixer(q_raw, k_raw, v_raw, i_raw, f_raw, o_raw, norm_g):
    b, s, _ = q_raw.shape
    f32 = jnp.float32
    q = to_chunks(q_raw.astype(f32) * (C_DK ** -0.5), C_HEADS)
    k = to_chunks(k_raw.astype(f32), C_HEADS)
    v = to_chunks(v_raw.astype(f32), C_HEADS)
    ig = to_chunks(i_raw.astype(f32), C_HEADS)[..., 0]
    lf = to_chunks(jax.nn.log_sigmoid(f_raw.astype(f32)), C_HEADS)[..., 0]
    mask = jnp.tril(jnp.ones((CHUNK, CHUNK), dtype=bool))

    def step(carry, inp):
        cmat, nvec, m = carry
        qt, kt, vt, it, ft = inp
        cum = jnp.cumsum(ft, axis=-1)
        log_intra = jnp.where(mask, cum[..., :, None] - cum[..., None, :] + it[..., None, :], NEG)
        log_inter = cum + m[..., None]
        m_t = jnp.maximum(log_inter, jnp.max(log_intra, axis=-1))
        dmat = jnp.exp(log_intra - m_t[..., None])
        inter = jnp.exp(log_inter - m_t)
        sc = jnp.einsum('bhtd,bhsd->bhts', qt, kt) * dmat
        num = jnp.einsum('bhts,bhsv->bhtv', sc, vt) + inter[..., None] * jnp.einsum('bhtd,bhdv->bhtv', qt, cmat)
        den = jnp.sum(sc, axis=-1) + inter * jnp.einsum('bhtd,bhd->bht', qt, nvec)
        h = num / jnp.maximum(jnp.abs(den), jnp.exp(-m_t))[..., None]
        m_new = m_t[..., -1]
        w_end = jnp.exp(cum[..., -1:] - cum + it - m_new[..., None])
        dec = jnp.exp(cum[..., -1] + m - m_new)
        cmat = dec[..., None, None] * cmat + jnp.einsum('bhs,bhsd,bhsv->bhdv', w_end, kt, vt)
        nvec = dec[..., None] * nvec + jnp.einsum('bhs,bhsd->bhd', w_end, kt)
        return (cmat, nvec, m_new), h

    c0 = (jnp.zeros((b, C_HEADS, C_DK, C_DV), f32), jnp.zeros((b, C_HEADS, C_DK), f32),
          jnp.zeros((b, C_HEADS), f32))
    _, h = lax.scan(step, c0, (q, k, v, ig, lf))
    h = head_rms_norm(from_chunks(h), norm_g, C_HEADS)
    return h * jax.nn.sigmoid(o_raw.astype(f32))

def hybrid_layer(x, norm_g, w_in, conv_w, conv_b, lb, hgrn_norm_g, attn_sinks,
                 mlstm_gate_b, mlstm_norm_g, w_mg, b_mg, w_br, w_out, pos):
    b, s, _ = x.shape
    dt = x.dtype
    h = rms_norm(x, norm_g)
    proj = jnp.einsum('bsd,dn->bsn', h, w_in)
    split_idx = np.cumsum(SPLIT_SIZES)[:-1].tolist()
    (a_q, a_f, a_i, a_z, b_q, b_k, b_v, b_z,
     c_qk, c_v, c_if, c_o, c_z) = jnp.split(proj, split_idx, axis=-1)
    u_a = (hgrn2_mixer(a_q, a_f, a_i, lb, hgrn_norm_g) * jax.nn.silu(a_z.astype(jnp.float32))).astype(dt)
    u_b = (swa_sink_attention(b_q, b_k, b_v, attn_sinks, pos) * jax.nn.silu(b_z)).astype(dt)
    c_qk = jax.nn.silu(causal_depthwise_conv(c_qk, conv_w, conv_b))
    c_q, c_k = jnp.split(c_qk, 2, axis=-1)
    c_if = c_if + mlstm_gate_b.astype(dt)
    u_c = (mlstm_mixer(c_q, c_k, c_v, c_if[..., :C_HEADS], c_if[..., C_HEADS:], c_o, mlstm_norm_g)
           * jax.nn.silu(c_z.astype(jnp.float32))).astype(dt)
    gates = jax.nn.sigmoid(jnp.einsum('bsd,dn->bsn', h, w_mg) + b_mg).reshape(b, s, N_BRANCH, D_MODEL)
    merged = (gates[:, :, 0] * jnp.einsum('bsw,wd->bsd', u_a, w_br[0])
              + gates[:, :, 1] * jnp.einsum('bsw,wd->bsd', u_b, w_br[1])
              + gates[:, :, 2] * jnp.einsum('bsw,wd->bsd', u_c, w_br[2]))
    return x + jnp.einsum('bsd,de->bse', merged.astype(dt), w_out)

def setup_inputs(seed: int = 0) -> dict:
    key = jax.random.key(seed)
    ks = jax.random.split(key, 16)
    f32 = jnp.float32
    nrm = lambda k, shp, sc: jax.random.normal(k, shp, f32) * sc
    f_bias = jnp.broadcast_to(jnp.linspace(3.0, 6.0, C_HEADS, dtype=f32), (DEPTH, C_HEADS))
    mlstm_gate_b = jnp.concatenate([nrm(ks[8], (DEPTH, C_HEADS), 0.1),
                                    f_bias + nrm(ks[9], (DEPTH, C_HEADS), 0.1)], axis=-1)
    return {
        "x": nrm(ks[0], (BATCH, SEQ, D_MODEL), 1.0),
        "norm_g": 1.0 + nrm(ks[1], (DEPTH, D_MODEL), 0.02),
        "w_in": nrm(ks[2], (DEPTH, D_MODEL, N_IN), D_MODEL ** -0.5),
        "conv_w": nrm(ks[3], (DEPTH, CONV_W, 2 * C_HEADS * C_DK), CONV_W ** -0.5),
        "conv_b": nrm(ks[4], (DEPTH, 2 * C_HEADS * C_DK), 0.01),
        "hgrn_lb": nrm(ks[5], (DEPTH, A_HEADS * A_DK), 0.5),
        "hgrn_norm_g": 1.0 + nrm(ks[6], (DEPTH, A_DV), 0.02),
        "attn_sinks": nrm(ks[7], (DEPTH, B_HEADS), 0.5),
        "mlstm_gate_b": mlstm_gate_b,
        "mlstm_norm_g": 1.0 + nrm(ks[10], (DEPTH, C_HEADS * C_DV), 0.02),
        "w_mg": nrm(ks[11], (DEPTH, D_MODEL, N_BRANCH * D_MODEL), D_MODEL ** -0.5),
        "b_mg": nrm(ks[12], (DEPTH, N_BRANCH * D_MODEL), 0.01),
        "w_br": nrm(ks[13], (DEPTH, N_BRANCH, BR_WIDTH, D_MODEL), BR_WIDTH ** -0.5),
        "w_out": nrm(ks[14], (DEPTH, D_MODEL, D_MODEL), D_MODEL ** -0.5),
        "final_g": 1.0 + nrm(ks[15], (D_MODEL,), 0.02),
    }

def reference(x, norm_g, w_in, conv_w, conv_b, hgrn_lb, hgrn_norm_g, attn_sinks,
              mlstm_gate_b, mlstm_norm_g, w_mg, b_mg, w_br, w_out, final_g):
    pos = jnp.arange(x.shape[1], dtype=jnp.int32)
    p = jax.nn.softmax(hgrn_lb.astype(jnp.float32), axis=0)
    lower_bounds = jnp.cumsum(p, axis=0) - p[0:1]
    for l in range(DEPTH):
        x = hybrid_layer(x, norm_g[l], w_in[l], conv_w[l], conv_b[l], lower_bounds[l],
                         hgrn_norm_g[l], attn_sinks[l], mlstm_gate_b[l], mlstm_norm_g[l],
                         w_mg[l], b_mg[l], w_br[l], w_out[l], pos)
    return rms_norm(x, final_g)


_drawn_inputs = setup_inputs


def setup_inputs(seed=0):
    import zlib

    import numpy as np

    out = dict(_drawn_inputs(seed))
    spreads = {}
    factors = {'norm_g': 3.284,
     'conv_b': 32.382,
     'hgrn_lb': 3.288,
     'hgrn_norm_g': 6.184,
     'attn_sinks': 64.0,
     'mlstm_norm_g': 8.0,
     'b_mg': 8.0,
     'final_g': 8.196}
    for name, (base, spread) in spreads.items():
        noise = np.random.default_rng([zlib.crc32(name.encode()), seed]).standard_normal(out[name].shape)
        drawn = base * np.exp(spread * noise) if base else spread * noise
        out[name] = __import__('jax').numpy.asarray(drawn.astype(out[name].dtype))
    for name, factor in factors.items():
        out[name] = (out[name] * factor).astype(out[name].dtype)
    return out
```

```python
from contextlib import ExitStack

import numpy as np

import concourse.bass as bass
from concourse import mybir

F32 = mybir.dt.float32
F32R = mybir.dt.float32r
I32 = mybir.dt.int32
ALU = mybir.AluOpType
ACT = mybir.ActivationFunctionType
AX = mybir.AxisListType.X

P = 128
DEPTH = 2
D = 1024
T = 1024
KB = D // P
NT = T // P
HALF = 512
HEADS = 4
BR = 512
CHUNK = 64
EPS = 1e-6
TINY = 1e-30
NEG = -1e30
SCALE = float(P) ** -0.5
SCALE_B = float(CHUNK) ** -0.5
THETA = 500000.0
LEVELS = 7

AQ, AF, AI, AZ, BQ, BK, BV, BZ = 0, 512, 1024, 1536, 2048, 2560, 2688, 2816
CQ, CK, CV, CIF, CO, CZ = 3328, 3840, 4352, 4864, 4872, 5384

RING = 3
BEHIND = (2, 2, 3)

C_ID, C_ONE, C_ROT, C_NEG, C_LVL = 0, 128, 256, 384, 512
C_COS = C_LVL + 64 * LEVELS
C_SIN = C_COS + T
C_END = C_SIN + T

R_CW, R_CB, R_LB, R_CG, R_AG, R_NG, R_FG, R_END = 0, 64, 80, 88, 96, 98, 114, 122

PHASES = {"pro": 1, "head": 4, "mid": 1, "branch": 3, "merge": 12, "join": 1, "out": 4}
OWN = {"pool": {"pro": 3, "head": 11, "merge": 3, "out": 2},
       "act": {"pro": 4, "head": 7},
       "dve": {"pro": 17, "head": 100, "merge": 2}}


class Event:

    def __init__(self, sem, first, per, by):
        self.sem, self.first, self.per, self.by = sem, first, per, by
        self.layer = sum(per.get(p, 0) * n for p, n in PHASES.items())

    def at(self, here, k):
        phase, layer, index = here
        before = 0
        for p, n in PHASES.items():
            if p == phase:
                break
            before += self.per.get(p, 0) * n
        assert self.first + before + k > 0, "a wait against a register's value stays positive"
        value = layer * (self.layer * self.by) + (self.first + before + k) * self.by
        if self.per.get(phase, 0) and not (isinstance(index, int) and index == 0):
            value = value + index * (self.per[phase] * self.by)
        return self.sem, value


def constants():
    c = np.zeros((P, C_END), np.float32)
    k = np.arange(P)
    c[:, C_ID:C_ID + P] = np.eye(P)
    c[:, C_ONE:C_ONE + P] = 1.0
    rot = np.zeros((P, P), np.float32)
    for m in range(P):
        r = m % CHUNK
        if r < 8:
            rot[m + 8, m] = -1.0
        elif r < 16:
            rot[m - 8, m] = 1.0
    c[:, C_ROT:C_ROT + P] = rot
    c[:, C_NEG:C_NEG + P] = np.where(k[:, None] > k[None, :], NEG, 0.0)
    for n in range(LEVELS):
        h = 64 >> n
        j = np.arange(64)
        block = j // h
        c[:, C_LVL + 64 * n:C_LVL + 64 * n + 64] = (k[:, None] // (2 * h) == block[None, :]) & (k[:, None] % (2 * h) < h)
    inv = np.float32(THETA) ** (-np.arange(8, dtype=np.float32) / 8)
    ang = np.arange(T, dtype=np.float32)[None, :] * inv[:, None]
    cos, sin = np.ones((P, T), np.float32), np.zeros((P, T), np.float32)
    for m in range(P):
        r = m % CHUNK
        if r < 16:
            cos[m], sin[m] = np.cos(ang[r % 8]), np.sin(ang[r % 8])
    c[:, C_COS:C_COS + T], c[:, C_SIN:C_SIN + T] = cos, sin
    dup = np.zeros((P, 4, P), np.float32)
    for g in range(2):
        for m in range(P):
            dup[CHUNK * g + m % CHUNK, g, m] = 1.0
        dup[:, 2 + g] = dup[:, g] @ rot
    return c, dup.reshape(P, 4 * P)


def tiles(ap):
    return ap.rearrange("p (t c) -> p t c", c=P)


def build(nc, x, norm_g, w_in, conv_w, conv_b, hgrn_lb, hgrn_norm_g, attn_sinks, mlstm_gate_b,
          mlstm_norm_g, w_mg, b_mg, w_br, w_out, final_g, consts, dups, out):
    ctx = ExitStack()
    with ctx:
        base = [-(-nc.sbuf_base // 64) * 64]

        def place(name, cols, dt=F32, at=None):
            t = nc.alloc_sbuf_tensor_at(name, [P, cols], dt, offset=base[0] if at is None else at)
            if at is None:
                base[0] += -(-cols // 8) * 32
            return t[:, :]

        raw = [place(f"w_raw{s}", D) for s in range(RING)]
        whi = [place(f"w_hi{s}", D, F32R) for s in range(RING)]
        wlo = [place(f"w_lo{s}", D, F32R) for s in range(RING)]
        hhi = place("h_hi", KB * T, F32R).rearrange("p (k t) -> p k t", k=KB)
        hlo = place("h_lo", KB * T, F32R).rearrange("p (k t) -> p k t", k=KB)
        slots_at = base[0]
        slots = place("slots", 23 * T).rearrange("p (s t) -> p s t", t=T)
        uhi = place("u_hi", 4 * T, F32R, slots_at + 4 * T * 4).rearrange("p (k t) -> p k t", k=4)
        ulo = place("u_lo", 4 * T, F32R, slots_at + 8 * T * 4).rearrange("p (k t) -> p k t", k=4)
        cst = place("constant_table", C_END)
        prm = place("parameter_columns", R_END)
        bmg = place("b_mg_columns", DEPTH * 24)
        hp = place("head_parameters", 16)
        ng = place("norm_g_columns", KB)
        sinks_all = place("sinks_everywhere", 16)
        sinks = place("sink_columns", 8)
        bcol = place("b_columns", 32)
        wcol = place("w_end_columns", 32)
        dec = place("decays", 32)
        nst = place("n_states", NT)
        small = place("small", 16 * 5)
        gb = place("gate_bias", 2)
        assert base[0] <= nc.sbuf_usable_end, base[0] - nc.sbuf_usable_end

        ident = cst[:, C_ID:C_ID + P]
        ones = cst[:, C_ONE:C_ONE + P]
        rotm = cst[:, C_ROT:C_ROT + P]
        negm = cst[:, C_NEG:C_NEG + P]
        cos, sin = cst[:, C_COS:C_COS + T], cst[:, C_SIN:C_SIN + T]

        def S(n):
            return slots[:, n, :]

        aq, ak, avt, cq, ck, cvt, bq, z0, z1, z2 = (S(n) for n in range(10))
        ast, cst_v = avt, cvt
        W = [S(10 + n) for n in range(9)]
        kd = [S(19), S(20)]
        vtok, vsh = S(21), S(22)
        xs = slots[:, 0:8, :]
        us = slots[:, 0:4, :]
        mg = slots[:, 12:20, :]
        ga = [S(20), S(21)]
        gt = S(22)

        psum = ctx.enter_context(nc.psum_tensor("psum", [P, 8 * HALF], F32))
        dense = [psum[:, 0:T], psum[:, T:2 * T]]
        mb = [psum[:, 2 * T + n * HALF:2 * T + (n + 1) * HALF] for n in range(4)]
        m01, m23 = psum[:, 2 * T:3 * T], psum[:, 3 * T:4 * T]

        x_d = nc.dram_tensor("x_feature_major", [KB, P, T], F32, kind="Internal").ap()
        u_d = nc.dram_tensor("branch_outputs", [3, HEADS, P, T], F32, kind="Internal").ap()
        row_d = nc.dram_tensor("gate_rows", [5, HEADS, T], F32, kind="Internal").ap()
        dec_d = nc.dram_tensor("decay_rows", [1, HEADS * NT], F32, kind="Internal").ap()

        def event(name, first=0, by=1, **per):
            return Event(ctx.enter_context(nc.semaphore(name)), first, per, by)

        landed = [event(f"w_landed{s}", by=16, pro=1, head=(4, 4, 3)[s], merge=1, out=(1, 1, 0)[s]) for s in range(RING)]
        split = event("w_split", first=2, pro=3, head=11, merge=3, out=2)
        block_done = event("block_done", first=2, pro=3, head=11, merge=3, out=2)
        emptied = [event("dense0_emptied", first=1, pro=2, head=6, merge=1, out=1),
                   event("dense1_emptied", first=1, pro=1, head=5, merge=1, out=1)]
        setup_in = event("setup_landed", by=16)
        setup_t = event("setup_transposed")
        setup_c = event("setup_copied")
        x_in = [event("x_landed0", by=16), event("x_landed1", by=16)]
        x_t = event("x_transposed")
        x_c = event("x_copied")
        x_ready = event("x_ready", first=1, out=2)
        sq = event("squared", pro=8)
        sq_sum = event("squares_summed", pro=8)
        ssq = event("sum_broadcast", pro=1)
        rstd = event("rstd_ready", pro=1)
        hn = event("h_normalised", pro=8)
        h_hi = event("h_hi_ready", pro=8)
        h_lo = event("h_lo_ready", pro=8)
        dup_in = event("dups_landed", by=16, pro=1)
        k_copied = event("k_copied", pro=1)
        k_rot = event("k_duplicated", pro=4)
        k_cos = event("k_duplicate_read", pro=4)
        kd_done = event("keys_ready", pro=2)
        v_copied = event("v_copied", pro=1)
        v_t = event("v_transposed", pro=1)
        v_tok = event("v_by_token", pro=1)
        v_sh = event("v_shifted", first=1, by=16, pro=2)
        if_copied = event("gate_rows_copied", pro=1)
        f_moved = event("f_rows_moved", by=16, pro=1)
        r_abs = event("f_abs", pro=1)
        r_scan = event("rows_scanned", pro=1)
        r_sums = event("row_sums_ready", pro=1)
        r_inter = event("inter_rows", pro=1)
        r_dec = event("decay_rows_ready", pro=1)
        r_exp = event("rows_ready", pro=1)
        r_out = event("rows_stored", by=16, pro=6)
        r_in = event("rows_reloaded", by=16, pro=3)
        r_t = event("row_columns_transposed", pro=1)
        r_col = event("row_columns_ready", pro=1)
        hp_done = event("head_parameters_ready", head=1)
        b_q = event("b_q_copied", head=1)
        b_z = event("b_gate", head=1)
        b_rope = event("b_q_rotated", head=1)
        b_qr = event("b_q_ready", head=1)
        b_s = event("b_scores", head=4)
        b_d = event("b_shifted", head=4)
        b_e = event("b_exp", head=4)
        b_p = event("b_probs", head=4)
        b_pt = event("b_probs_transposed", head=4)
        b_ptc = event("b_probs_copied", head=4)
        b_o = event("b_out", head=4)
        b_done = event("b_done", first=1, head=1)
        b_st = event("b_stored", first=1, by=16, head=1)
        a_q = event("a_q", head=1)
        a_sig = event("a_sigmoid", head=1)
        a_f = event("a_f", head=1)
        a_ln = event("a_log_f", head=1)
        a_v = event("a_v_copied", head=1)
        a_vt = event("a_v_transposed", head=1)
        a_vtok = event("a_v_by_token", head=1)
        a_k = event("a_k", head=1)
        a_cum = event("a_cum", head=1)
        a_diff = event("a_decay_exponents", head=8)
        a_e = event("a_decays", head=9)
        a_kq = event("a_decayed", head=9)
        a_dg = event("a_diagonal", head=1)
        a_sa = event("a_diagonal_taken", head=2)
        a_lv = event("a_level", head=7)
        a_pr = event("a_level_taken", head=7)
        a_kt = event("a_k_transposed", head=1)
        a_ktc = event("a_k_by_token", head=1)
        a_u = event("a_updates", head=1)
        a_last = event("a_tile_exponents", head=1)
        a_el = event("a_tile_decays", head=1)
        a_st = event("a_states", head=1)
        a_o = event("a_out", head=1)
        a_oc = event("a_out_copied", head=1)
        a_sq = event("a_squared", head=1)
        a_ss = event("a_sum", head=1)
        a_rs = event("a_rstd", head=1)
        a_z = event("a_gate", head=1)
        a_done = event("a_done", first=1, head=1)
        a_stored = event("a_stored", first=1, by=16, head=1)
        c_qc = event("c_q_bias", head=1)
        c_kc = event("c_k_bias", head=1)
        c_qt = event("c_q_convolved", head=1)
        c_q = event("c_q", head=1)
        c_k = event("c_k", head=1)
        c_v = event("c_v_copied", head=1)
        c_in = event("c_rows_landed", by=16, head=3)
        c_vt = event("c_v_transposed", head=1)
        c_vtok = event("c_v_by_token", head=1)
        c_kt = event("c_k_transposed", head=1)
        c_kw = event("c_k_weighted", head=2)
        c_dx = event("c_dmat_exponents", head=1)
        c_dm = event("c_dmat", head=1)
        c_s = event("c_scores", head=1)
        c_sc = event("c_scores_weighted", head=2)
        c_qp = event("c_q_inter", head=1)
        c_u = event("c_updates", head=1)
        c_st = event("c_states", head=1)
        c_t = event("c_den_terms", head=1)
        c_o = event("c_num", head=1)
        c_den = event("c_den", head=1)
        c_ab = event("c_den_abs", head=1)
        c_mx = event("c_den_bounded", head=1)
        c_r = event("c_den_reciprocal", head=1)
        c_h = event("c_h", head=1)
        c_sq = event("c_squared", head=1)
        c_ss = event("c_sum", head=1)
        c_rs = event("c_rstd", head=1)
        c_zo = event("c_output_gate", head=1)
        c_zz = event("c_gate", head=1)
        c_done = event("c_done", first=1, head=1)
        c_stored = event("c_stored", first=1, by=16, head=1)
        cleared = event("merge_cleared", head=0, mid=1)
        u_in = event("u_landed", by=16, branch=1)
        u_hi = event("u_hi_ready", branch=4)
        u_lo = event("u_lo_ready", first=1, branch=4)
        g_sig = event("g_sigmoid", merge=2)
        br_done = event("branch_products", merge=1)
        br_taken = event("branch_taken", first=1, merge=2)
        m_hi = event("merged_hi", join=KB)
        m_lo = event("merged_lo", join=KB)
        xo_in = [event("x_old_landed0", by=16, out=1), event("x_old_landed1", by=16, out=1)]
        x_dst = event("x_stored", by=16, pro=1)
        fin = event("final_step")
        fin_t = event("final_transposed")
        fin_c = event("final_copied")
        fin_a = event("final_log")
        y_out = [event("y_stored0", by=16), event("y_stored1", by=16)]
        passed = ctx.enter_context(nc.semaphore("waits_passed"))
        own = {}
        for name, per in OWN.items():
            own[name] = event(name + "_step", **per)

        block = ctx.enter_context(nc.Block())

        def once(ev, k):
            return ev.sem, (ev.first + k) * ev.by

        def last(ev, k=0):
            return ev.sem, (ev.first + DEPTH * ev.layer + k) * ev.by

        def begin(eng, *events):
            for ev in events:
                eng.sem_inc(ev.sem, ev.first * ev.by)

        def plain(eng):
            eng.sem_inc(passed, 1)

        def layers(eng, pro, head, mid, branch, merge, join, outs, calm=False):
            with eng.Fori(0, DEPTH, 1) as layer:
                pro(("pro", layer, 0), layer)
                if calm:
                    plain(eng)
                with eng.Fori(0, 2, 1) as g:
                    with eng.Fori(0, 2, 1) as j:
                        i = g * 2 + j
                        head(("head", layer, i), layer, i, g)
                mid(("mid", layer, 0), layer)
                if calm:
                    plain(eng)
                with eng.Fori(0, 3, 1) as b:
                    branch(("branch", layer, b), ("merge", layer, b * 4), b)
                    if calm:
                        plain(eng)
                    with eng.Fori(0, 4, 1) as d:
                        merge(("merge", layer, b * 4 + d), layer, b, d)
                join(("join", layer, 0), layer)
                if calm:
                    plain(eng)
                with eng.Fori(0, 4, 1) as e:
                    outs(("out", layer, e), layer, e)

        def nothing(*_):
            pass

        @block.sync
        def _(sp):
            def load(here, j, src):
                sp.wait_ge(*split.at(here, j - BEHIND[min(j, 2)] + 1))
                s = j % RING
                sp.dma_start(raw[s].rearrange("p (k n) -> p k n", k=src.shape[1]), src).then_inc(landed[s].sem, 16)

            def cols(w, layer, c0, n=P):
                return w[bass.ds(layer, 1), :, bass.ds(c0, n)].rearrange("l (k p) n -> p (l k) n", p=P)

            def pro(here, layer):
                for j, c0 in enumerate((BK, BV, CIF)):
                    load(here, j, cols(w_in, layer, c0))

            def head(here, layer, i, g):
                for j, c0 in enumerate((BQ, BZ, AQ, AF, AI, CQ, CK, CV, AZ, CO, CZ)):
                    load(here, j, cols(w_in, layer, i * P + c0))

            def merge(here, layer, b, d):
                for j in range(2):
                    load(here, j, cols(w_mg, layer, b * D + d * 256 + j * P))
                src = w_br[bass.ds(layer, 1), bass.ds(b, 1), :, bass.ds(d * 256, 256)]
                load(here, 2, src.rearrange("l b (k p) n -> p (l b k) n", p=P))

            def outs(here, layer, e):
                for j in range(2):
                    load(here, j, cols(w_out, layer, e * 256 + j * P))

            layers(sp, pro, head, nothing, nothing, merge, nothing, outs)

        @block.gpsimd
        def _(pool):
            begin(pool, split)
            step = own["pool"]

            def halve(here, j):
                s = j % RING
                pool.wait_ge(*landed[s].at(here, j // RING + 1))
                pool.wait_ge(*block_done.at(here, j - BEHIND[min(j, 2)] + 1))
                plain(pool)
                pool.tensor_copy(whi[s], raw[s]).then_inc(step.sem, 1)
                pool.wait_ge(*step.at(here, j + 1))
                pool.tensor_tensor(wlo[s], raw[s], whi[s].bitcast(F32), ALU.subtract).then_inc(split.sem, 1)

            def body(n):
                def run(here, *rest):
                    for j in range(n):
                        halve(here, j)
                return run

            layers(pool, body(3), body(11), nothing, nothing, body(3), nothing, body(2))

        @block.tensor
        def _(pe):
            def transposes(src, dst, n0=0, n1=NT):
                for n in range(n0, n1):
                    ins = pe.transpose(dst[:, (n - n0) * P:(n - n0 + 1) * P], src[:, n * P:(n + 1) * P], ident)
                return ins

            def project(here, j, kk, hi, lo, dst, w0=0, step=P):
                s = j % RING
                for half in range(2):
                    t = slice(half * HALF, (half + 1) * HALF)
                    n = 0
                    for k in range(kk):
                        w = slice(k * step + w0, k * step + w0 + P)
                        for ww, xx in ((whi[s], hi), (wlo[s], hi), (whi[s], lo)):
                            ins = pe.matmul(dst[:, t], ww[:, w], xx[:, k, t], start=(n == 0), stop=(n == 3 * kk - 1))
                            n += 1
                return ins

            def wait_block(here, j, d, k):
                pe.wait_ge(*split.at(here, j + 1))
                pe.wait_ge(*emptied[d].at(here, k))

            begin(pe, block_done)
            pe.wait_ge(*once(setup_in, 12))
            pe.transpose(m01[:, 0:R_END], W[8][0:R_END, 0:P], ident[0:R_END, 0:R_END])
            pe.transpose(m01[:, 128:128 + DEPTH * 24], W[8][0:DEPTH * 24, P:2 * P], ident[0:DEPTH * 24, 0:DEPTH * 24]).then_inc(setup_t.sem, 1)
            for n in range(NT):
                pe.wait_ge(*once(x_in[n % 2], n // 2 + 1))
                if n >= 2:
                    pe.wait_ge(*once(x_c, n - 1))
                dst = dense[n % 2]
                src = W[n % 2]
                for k in range(KB):
                    ins = pe.transpose(dst[:, k * P:(k + 1) * P], src[:, k * P:(k + 1) * P], ident)
                ins.then_inc(x_t.sem, 1)
            pe.wait_ge(*once(x_c, NT))

            def pro(here, layer):
                pe.wait_ge(*sq_sum.at(here, 8))
                for half in range(2):
                    ins = pe.matmul(m01[:, half * HALF:(half + 1) * HALF], ones, W[0][:, half * HALF:(half + 1) * HALF], start=True, stop=True)
                ins.then_inc(ssq.sem, 1)
                pe.wait_ge(*h_lo.at(here, 8))
                wait_block(here, 0, 0, 0)
                project(here, 0, KB, hhi, hlo, dense[0]).then_inc(block_done.sem, 1)
                wait_block(here, 1, 1, 0)
                project(here, 1, KB, hhi, hlo, dense[1]).then_inc(block_done.sem, 1)
                pe.wait_ge(*k_copied.at(here, 1))
                pe.wait_ge(*dup_in.at(here, 1))
                for g in range(2):
                    for r in range(2):
                        if g:
                            pe.wait_ge(*k_cos.at(here, r + 1))
                        dst = (m01, m23)[r]
                        for half in range(2):
                            ins = pe.matmul(dst[:, half * HALF:(half + 1) * HALF], z2[:, (2 * r + g) * P:(2 * r + g + 1) * P],
                                            W[0][:, half * HALF:(half + 1) * HALF], start=True, stop=True)
                        ins.then_inc(k_rot.sem, 1)
                wait_block(here, 2, 0, 1)
                project(here, 2, KB, hhi, hlo, dense[0]).then_inc(block_done.sem, 1)
                pe.wait_ge(*v_copied.at(here, 1))
                pe.wait_ge(*k_cos.at(here, 4))
                transposes(W[2], m01).then_inc(v_t.sem, 1)
                pe.wait_ge(*r_in.at(here, 3))
                plain(pe)
                pe.transpose(mb[2][:, 0:32], z0[0:32, 0:P], ident[0:32, 0:32])
                pe.transpose(mb[2][:, 32:64], z0[0:32, P:2 * P], ident[0:32, 0:32]).then_inc(r_t.sem, 1)

            def head(here, layer, i, g):
                def dense_block(j):
                    wait_block(here, j, j % 2, j // 2)
                    project(here, j, KB, hhi, hlo, dense[j % 2]).then_inc(block_done.sem, 1)

                def level(n):
                    h = 64 >> n
                    if n < 2:
                        pe.wait_ge(*a_vtok.at(here, 1))
                    else:
                        pe.wait_ge(*a_pr.at(here, n - 1))
                    pe.wait_ge(*a_kq.at(here, n + 1))
                    kq = W[2 + n % 3]
                    for t in range(NT):
                        tile = kq[:, t * P:(t + 1) * P]
                        ins = pe.matmul(mb[n % 2][:, t * 64:(t + 1) * 64], tile,
                                        tile.rearrange("p (b e) -> p b e", e=2 * h)[:, :, h:2 * h], start=True, stop=True)
                    ins.then_inc(a_lv.sem, 1)

                dense_block(0)
                dense_block(1)
                pe.wait_ge(*b_q.at(here, 1))
                pe.wait_ge(*c_done.at(here, 0))
                for half in range(2):
                    t = slice(half * HALF, (half + 1) * HALF)
                    ins = pe.matmul(m01[:, t], rotm, bq[:, t], start=True, stop=True)
                ins.then_inc(b_rope.sem, 1)
                dense_block(2)
                pe.wait_ge(*b_qr.at(here, 1))
                plain(pe)
                for q in range(4):
                    for c in range(4):
                        n = 4 * q + c
                        k0 = CHUNK * max(n - 1, 0)
                        for h in range(2):
                            r = slice(h * CHUNK, (h + 1) * CHUNK)
                            ins = pe.matmul(mb[q][r, c * P:(c + 1) * P], bq[r, n * CHUNK:(n + 1) * CHUNK],
                                            W[6][r, k0:k0 + P], start=True, stop=True)
                    ins.then_inc(b_s.sem, 1)
                dense_block(3)
                for q in range(4):
                    pe.wait_ge(*b_p.at(here, q + 1))
                    transposes(W[q // 2], mb[q], (q % 2) * 4, (q % 2) * 4 + 4).then_inc(b_pt.sem, 1)
                dense_block(4)
                for q in range(4):
                    pe.wait_ge(*b_ptc.at(here, q + 1))
                    for c in range(4):
                        n = 4 * q + c
                        if n == 0:
                            v = W[4][:, 0:P]
                        elif n % 2:
                            v = W[4][:, (n // 2) * P:(n // 2 + 1) * P]
                        else:
                            v = W[5][:, (n // 2 - 1) * P:(n // 2) * P]
                        ins = pe.matmul(mb[q][:, c * P:(c + 1) * P], v, W[2 + q // 2][:, (n % 8) * P:(n % 8 + 1) * P], start=True, stop=True)
                    ins.then_inc(b_o.sem, 1)
                dense_block(5)
                pe.wait_ge(*a_v.at(here, 1))
                pe.wait_ge(*b_done.at(here, 1))
                transposes(avt, m01).then_inc(a_vt.sem, 1)
                pe.wait_ge(*a_k.at(here, 1))
                for t in range(NT):
                    c = slice(t * P, (t + 1) * P)
                    ins = pe.matmul(m23[:, c], ak[:, c], aq[:, c], start=True, stop=True)
                ins.then_inc(a_dg.sem, 1)
                for n in range(3):
                    level(n)
                dense_block(6)
                for n in range(3, 7):
                    level(n)
                pe.wait_ge(*a_kq.at(here, 8))
                pe.wait_ge(*a_sa.at(here, 2))
                transposes(W[3], m23).then_inc(a_kt.sem, 1)
                dense_block(7)
                pe.wait_ge(*a_ktc.at(here, 1))
                pe.wait_ge(*a_pr.at(here, 7))
                for t in range(NT - 1):
                    c = slice(t * P, (t + 1) * P)
                    ins = pe.matmul(m01[:, c], W[0][:, c], W[7][:, c], start=True, stop=True)
                ins.then_inc(a_u.sem, 1)
                dense_block(8)
                pe.wait_ge(*a_st.at(here, 1))
                pe.wait_ge(*a_kq.at(here, 9))
                for t in range(NT):
                    c = slice(t * P, (t + 1) * P)
                    ins = pe.matmul(m23[:, c], W[7][:, c], W[6][:, c], start=True, stop=(t == 0))
                    if t:
                        ins = pe.matmul(m23[:, c], ast[:, c], W[5][:, c], start=False, stop=True)
                ins.then_inc(a_o.sem, 1)
                dense_block(9)
                pe.wait_ge(*a_sq.at(here, 1))
                for half in range(2):
                    t = slice(half * HALF, (half + 1) * HALF)
                    ins = pe.matmul(m01[:, t], ones, W[2][:, t], start=True, stop=True)
                ins.then_inc(a_ss.sem, 1)
                pe.wait_ge(*c_v.at(here, 1))
                pe.wait_ge(*a_oc.at(here, 1))
                transposes(cvt, m23).then_inc(c_vt.sem, 1)
                pe.wait_ge(*c_k.at(here, 1))
                pe.wait_ge(*a_rs.at(here, 1))
                transposes(ck, m01).then_inc(c_kt.sem, 1)
                pe.wait_ge(*c_vtok.at(here, 1))
                pe.wait_ge(*c_q.at(here, 1))
                for t in range(NT):
                    c = slice(t * P, (t + 1) * P)
                    ins = pe.matmul(m23[:, c], ck[:, c], cq[:, c], start=True, stop=True)
                ins.then_inc(c_s.sem, 1)
                dense_block(10)
                pe.wait_ge(*c_kw.at(here, 2))
                pe.wait_ge(*c_sc.at(here, 2))
                for t in range(NT - 1):
                    c = slice(t * P, (t + 1) * P)
                    pe.matmul(m01[:, c], W[6][:, c], W[5][:, c], start=True, stop=True)
                    ins = pe.matmul(m23[:, 2 * t:2 * t + 2], W[6][:, c], ones[:, 0:2], start=True, stop=True)
                ins.then_inc(c_u.sem, 1)
                pe.wait_ge(*c_st.at(here, 1))
                pe.wait_ge(*c_t.at(here, 1))
                for half in range(2):
                    t = slice(half * HALF, (half + 1) * HALF)
                    ins = pe.matmul(m01[:, t], ones, W[2][:, t], start=True, stop=True)
                ins.then_inc(c_den.sem, 1)
                for t in range(NT):
                    c = slice(t * P, (t + 1) * P)
                    ins = pe.matmul(m23[:, c], W[5][:, c], W[0][:, c], start=True, stop=(t == 0))
                    if t:
                        ins = pe.matmul(m23[:, c], cst_v[:, c], W[1][:, c], start=False, stop=True)
                ins.then_inc(c_o.sem, 1)
                pe.wait_ge(*c_sq.at(here, 1))
                for half in range(2):
                    t = slice(half * HALF, (half + 1) * HALF)
                    ins = pe.matmul(m01[:, t], ones, W[4][:, t], start=True, stop=True)
                ins.then_inc(c_ss.sem, 1)

            def merge(here, layer, b, d):
                for j in range(2):
                    wait_block(here, j, j, 0)
                    project(here, j, KB, hhi, hlo, dense[j]).then_inc(block_done.sem, 1)
                pe.wait_ge(*split.at(here, 3))
                pe.wait_ge(*u_lo.at(("branch", layer, b), 4))
                pe.wait_ge(*br_taken.at(here, 0))
                project(here, 2, 4, uhi, ulo, m01, 0, 256).then_inc(br_done.sem, 1)
                project(here, 2, 4, uhi, ulo, m23, P, 256).then_inc(block_done.sem, 1)

            def join(here, layer):
                pe.wait_ge(*m_lo.at(here, KB))

            def outs(here, layer, e):
                for j in range(2):
                    wait_block(here, j, j, 0)
                    project(here, j, KB, hhi, hlo, dense[j]).then_inc(block_done.sem, 1)

            layers(pe, pro, head, nothing, nothing, merge, join, outs, True)

            pe.wait_ge(*once(fin, 8))
            for half in range(2):
                ins = pe.matmul(m01[:, half * HALF:(half + 1) * HALF], ones, W[0][:, half * HALF:(half + 1) * HALF], start=True, stop=True)
            ins.then_inc(ssq.sem, 1)
            pe.wait_ge(*once(fin, 16))
            for n in range(NT):
                if n >= 2:
                    pe.wait_ge(*once(fin_c, n - 1))
                for k in range(KB):
                    ins = pe.transpose(dense[n % 2][:, k * P:(k + 1) * P], xs[:, k, n * P:(n + 1) * P], ident)
                ins.then_inc(fin_t.sem, 1)

        @block.scalar
        def _(act):
            step = own["act"]
            LNEXP = "natural_log_exp_and_others"

            begin(act, *emptied, b_st, a_stored, c_stored, v_sh)
            rows = W[8]
            loads = [
                (cst, consts),
                (rows[R_CW:R_CW + 64, 0:P], conv_w.rearrange("l w (j c) -> (l w j) c", c=P)),
                (rows[R_CB:R_CB + 16, 0:P], conv_b.rearrange("l (j c) -> (l j) c", c=P)),
                (rows[R_LB:R_LB + 8, 0:P], hgrn_lb.rearrange("l (j c) -> (l j) c", c=P)),
                (rows[R_CG:R_CG + 8, 0:P], mlstm_norm_g.rearrange("l (j c) -> (l j) c", c=P)),
                (rows[R_AG:R_AG + 2, 0:P], hgrn_norm_g),
                (rows[R_NG:R_NG + 16, 0:P], norm_g.rearrange("l (j c) -> (l j) c", c=P)),
                (rows[R_FG:R_FG + 8, 0:P], final_g.rearrange("(j c) -> j c", c=P)),
                (rows[0:DEPTH * 24, P:2 * P], b_mg.rearrange("l (j c) -> (l j) c", c=P)),
                (sinks_all, attn_sinks.rearrange("(o l) h -> o (l h)", o=1).partition_broadcast(P)),
                (gb[0:8, 0:1], mlstm_gate_b[0:1, :].rearrange("l h -> h l")),
                (gb[0:8, 1:2], mlstm_gate_b[1:2, :].rearrange("l h -> h l")),
            ]
            for dst, src in loads:
                act.dma_start(dst, src).then_inc(setup_in.sem, 16)
            act.preload_act_table_set(LNEXP)
            act.wait_ge(*once(setup_c, 4))
            act.activation(prm[:, R_LB:R_LB + 8], small[:, 16:24], ACT.Exp).then_inc(setup_c.sem, 1)
            for n in range(NT):
                if n >= 2:
                    act.wait_ge(*once(x_t, n - 1))
                act.dma_start(W[n % 2], x[0, n * P:(n + 1) * P, :]).then_inc(x_in[n % 2].sem, 16)
            act.wait_ge(*once(x_c, NT))

            def pro(here, layer):
                n = [0]

                def mine():
                    n[0] += 1
                    act.wait_ge(*step.at(here, n[0]))

                act.wait_ge(*x_ready.at(here, 0))
                act.dma_start(x_d.rearrange("k p t -> p k t"), xs).then_inc(x_dst.sem, 16)
                act.dma_start(z2[:, 0:4 * P], dups).then_inc(dup_in.sem, 16)
                for k in range(KB):
                    if k >= 2:
                        act.wait_ge(*sq_sum.at(here, k - 1))
                    act.activation(W[1 + k % 2], xs[:, k, :], ACT.Square).then_inc(sq.sem, 1)
                act.preload_act_table_set(LNEXP)
                act.wait_ge(*ssq.at(here, 1))
                act.activation(W[3], m01, ACT.Ln, bias=EPS, scale=1.0 / D).then_inc(step.sem, 1)
                mine()
                act.activation(W[3], W[3], ACT.Exp, scale=-0.5).then_inc(rstd.sem, 1)
                for k in range(KB):
                    act.wait_ge(*hn.at(here, k + 1))
                    act.activation(hhi[:, k, :], W[4 + k % 2], ACT.Copy).then_inc(h_hi.sem, 1)
                act.wait_ge(*h_lo.at(here, 8))
                act.wait_ge(*block_done.at(here, 1))
                act.activation(W[0], dense[0], ACT.Copy).then_inc(k_copied.sem, 1)
                act.wait_ge(*k_copied.at(here, 1))
                act.sem_inc(emptied[0].sem, 1)
                act.wait_ge(*block_done.at(here, 2))
                act.activation(W[2], dense[1], ACT.Copy).then_inc(v_copied.sem, 1)
                act.wait_ge(*v_copied.at(here, 1))
                act.sem_inc(emptied[1].sem, 1)
                act.wait_ge(*v_t.at(here, 1))
                act.activation(vtok, m01, ACT.Copy).then_inc(v_tok.sem, 1)
                act.wait_ge(*v_tok.at(here, 1))
                act.dma_start(vsh[0:64, 0:7 * P], vtok[64:128, 0:7 * P]).then_inc(v_sh.sem, 16)
                act.dma_start(vsh[64:128, 0:7 * P], vtok[0:64, P:8 * P]).then_inc(v_sh.sem, 16)
                act.wait_ge(*if_copied.at(here, 1))
                act.dma_start(W[4][0:4, :], W[3][4:8, :]).then_inc(f_moved.sem, 16)
                act.wait_ge(*f_moved.at(here, 1))
                act.activation(W[5][0:4, :], W[4][0:4, :], ACT.Abs).then_inc(step.sem, 1)
                mine()
                act.activation(W[5][0:4, :], W[5][0:4, :], ACT.Exp, scale=-1.0).then_inc(step.sem, 1)
                mine()
                act.activation(W[5][0:4, :], W[5][0:4, :], ACT.Ln, bias=1.0).then_inc(r_abs.sem, 1)
                act.wait_ge(*r_sums.at(here, 1))
                act.activation(W[6][0:4, :], W[6][0:4, :], ACT.Exp).then_inc(r_inter.sem, 1)
                act.activation(W[7][0:4, :], W[7][0:4, :], ACT.Exp, scale=-1.0).then_inc(step.sem, 1)
                mine()
                act.activation(W[5][0:4, :], W[5][0:4, :], ACT.Exp).then_inc(r_exp.sem, 1)
                act.wait_ge(*r_exp.at(here, 1))
                act.wait_ge(*r_dec.at(here, 1))
                for kind, src in enumerate((W[8], W[6], W[7], W[3], W[5])):
                    act.dma_start(row_d[kind], src[0:4, :]).then_inc(r_out.sem, 16)
                act.dma_start(dec_d.rearrange("o (h t) -> (o h) t", h=HEADS), small[0:4, 0:NT]).then_inc(r_out.sem, 16)
                act.wait_ge(*r_out.at(here, 6))
                act.wait_ge(*x_dst.at(here, 1))
                for kind in (3, 4):
                    act.dma_start(z0[0:32, (kind - 3) * P:(kind - 2) * P],
                                  row_d[kind].rearrange("h (t c) -> (h t) c", c=P)).then_inc(r_in.sem, 16)
                act.dma_start(dec, dec_d.partition_broadcast(P)).then_inc(r_in.sem, 16)

            def head(here, layer, i, g):
                n = [0]

                def mine():
                    n[0] += 1
                    act.wait_ge(*step.at(here, n[0]))

                def empty(j, ev, dst, func, **kw):
                    act.wait_ge(*block_done.at(here, j + 1))
                    act.activation(dst, dense[j % 2], func, **kw).then_inc(ev.sem, 1)

                def emptied_by(ev, j):
                    act.wait_ge(*ev.at(here, 1))
                    act.sem_inc(emptied[j % 2].sem, 1)

                empty(0, b_q, bq, ACT.Copy)
                emptied_by(b_q, 0)
                act.wait_ge(*a_done.at(here, 0))
                empty(1, b_z, z0, ACT.Silu)
                emptied_by(b_z, 1)
                empty(2, a_q, aq, ACT.Silu)
                emptied_by(a_q, 2)
                act.preload_act_table_set(LNEXP)
                for q in range(4):
                    act.wait_ge(*b_d.at(here, q + 1))
                    p = W[q // 2][:, (q % 2) * HALF:(q % 2 + 1) * HALF]
                    act.activation(p, p, ACT.Exp).then_inc(b_e.sem, 1)
                    act.activation(small[:, 32 + 4 * q:36 + 4 * q], small[:, 16 + 4 * q:20 + 4 * q], ACT.Exp).then_inc(step.sem, 1)
                    n[0] += 1
                empty(3, a_sig, ak, ACT.Sigmoid)
                emptied_by(a_sig, 3)
                for q in range(4):
                    act.wait_ge(*b_pt.at(here, q + 1))
                    act.activation(W[2 + q // 2][:, (q % 2) * HALF:(q % 2 + 1) * HALF], mb[q], ACT.Copy).then_inc(b_ptc.sem, 1)
                empty(4, a_v, avt, ACT.Copy)
                emptied_by(a_v, 4)
                act.preload_act_table_set(LNEXP)
                act.wait_ge(*b_done.at(here, 1))
                act.dma_start(u_d[1, bass.ds(i, 1)].rearrange("o p t -> p (o t)"), W[8]).then_inc(b_st.sem, 16)
                act.wait_ge(*a_f.at(here, 1))
                act.activation(W[0], W[0], ACT.Ln).then_inc(a_ln.sem, 1)

                def decay(m):
                    act.wait_ge(*a_diff.at(here, m + 1))
                    act.activation(W[2 + m % 3], W[2 + m % 3], ACT.Exp).then_inc(a_e.sem, 1)

                def tap(j, ev, dst, col):
                    act.wait_ge(*block_done.at(here, j + 1))
                    act.wait_ge(*c_done.at(here, 0))
                    act.wait_ge(*hp_done.at(here, 1))
                    act.activation(dst, dense[j % 2], ACT.Identity, bias=hp[:, col + 8:col + 9], scale=hp[:, col + 6:col + 7]).then_inc(ev.sem, 1)

                decay(0)
                tap(5, c_qc, cq, 0)
                act.wait_ge(*a_vt.at(here, 1))
                act.activation(W[7], m01, ACT.Copy).then_inc(a_vtok.sem, 1)
                for m in range(1, 8):
                    decay(m)
                act.activation(W[5], W[1], ACT.Exp).then_inc(a_e.sem, 1)
                tap(6, c_kc, ck, 1)
                act.wait_ge(*a_last.at(here, 1))
                act.activation(small[:, NT:2 * NT], small[:, 0:NT], ACT.Exp).then_inc(a_el.sem, 1)
                act.wait_ge(*a_kt.at(here, 1))
                act.activation(W[0], m23, ACT.Copy).then_inc(a_ktc.sem, 1)
                empty(7, c_v, cvt, ACT.Copy)
                emptied_by(c_v, 7)
                act.wait_ge(*c_qt.at(here, 1))
                act.activation(cq, cq, ACT.Silu).then_inc(c_q.sem, 1)
                act.wait_ge(*emptied[0].at(here, 4))
                act.activation(ck, ck, ACT.Silu).then_inc(c_k.sem, 1)
                act.wait_ge(*b_done.at(here, 1))
                empty(8, a_z, z0, ACT.Silu)
                emptied_by(a_z, 8)
                act.wait_ge(*a_o.at(here, 1))
                act.activation(W[4], m23, ACT.Copy).then_inc(a_oc.sem, 1)
                act.wait_ge(*a_oc.at(here, 1))
                act.activation(W[2], W[4], ACT.Square).then_inc(a_sq.sem, 1)
                act.dma_start(W[0], row_d[0, bass.ds(i, 1), :].partition_broadcast(P)).then_inc(c_in.sem, 16)
                act.dma_start(W[1], row_d[1, bass.ds(i, 1), :].partition_broadcast(P)).then_inc(c_in.sem, 16)
                act.dma_start(W[7], row_d[2, bass.ds(i, 1), :].partition_broadcast(P)).then_inc(c_in.sem, 16)
                empty(9, c_zo, z1, ACT.Sigmoid)
                emptied_by(c_zo, 9)
                act.preload_act_table_set(LNEXP)
                act.wait_ge(*a_ss.at(here, 1))
                act.activation(W[3], m01, ACT.Ln, bias=EPS, scale=1.0 / P).then_inc(step.sem, 1)
                mine()
                act.activation(W[3], W[3], ACT.Exp, scale=-0.5).then_inc(a_rs.sem, 1)
                act.wait_ge(*c_vt.at(here, 1))
                act.activation(W[5], m23, ACT.Copy).then_inc(c_vtok.sem, 1)
                act.wait_ge(*c_dx.at(here, 1))
                act.activation(W[0], W[0], ACT.Exp).then_inc(c_dm.sem, 1)
                act.wait_ge(*a_done.at(here, 1))
                act.dma_start(u_d[0, bass.ds(i, 1)].rearrange("o p t -> p (o t)"), W[8]).then_inc(a_stored.sem, 16)
                empty(10, c_zz, z2, ACT.Silu)
                emptied_by(c_zz, 10)
                act.preload_act_table_set(LNEXP)
                act.wait_ge(*c_den.at(here, 1))
                act.activation(W[3], m01, ACT.Abs).then_inc(c_ab.sem, 1)
                act.wait_ge(*c_mx.at(here, 1))
                act.activation(W[3], W[3], ACT.Ln).then_inc(step.sem, 1)
                mine()
                act.activation(W[3], W[3], ACT.Exp, scale=-1.0).then_inc(c_r.sem, 1)
                act.wait_ge(*c_h.at(here, 1))
                act.activation(W[4], W[8], ACT.Square).then_inc(c_sq.sem, 1)
                act.wait_ge(*c_ss.at(here, 1))
                act.activation(W[3], m01, ACT.Ln, bias=EPS, scale=1.0 / P).then_inc(step.sem, 1)
                mine()
                act.activation(W[3], W[3], ACT.Exp, scale=-0.5).then_inc(c_rs.sem, 1)
                act.wait_ge(*c_done.at(here, 1))
                act.dma_start(u_d[2, bass.ds(i, 1)].rearrange("o p t -> p (o t)"), W[8]).then_inc(c_stored.sem, 16)
                assert n[0] == OWN["act"]["head"], n

            def branch(here, merging, b):
                act.wait_ge(*a_stored.at(here, 0))
                act.wait_ge(*b_st.at(here, 0))
                act.wait_ge(*c_stored.at(here, 0))
                act.wait_ge(*block_done.at(merging, 0))
                act.wait_ge(*u_lo.at(here, 0))
                act.dma_start(us, u_d[bass.ds(b, 1)].rearrange("b k p t -> p (b k) t")).then_inc(u_in.sem, 16)
                act.wait_ge(*u_in.at(here, 1))
                for k in range(4):
                    act.activation(uhi[:, k, :], us[:, k, :], ACT.Copy).then_inc(u_hi.sem, 1)

            def merge(here, layer, b, d):
                for j in range(2):
                    act.wait_ge(*block_done.at(here, j + 1))
                    act.wait_ge(*br_taken.at(here, 0))
                    act.activation(ga[j], dense[j], ACT.Sigmoid, bias=bmg[:, bass.ds(layer * 24 + b * 8 + d * 2 + j, 1)]).then_inc(g_sig.sem, 1)
                    act.wait_ge(*g_sig.at(here, j + 1))
                    act.sem_inc(emptied[j].sem, 1)

            def join(here, layer):
                act.wait_ge(*br_taken.at(here, 0))
                for k in range(KB):
                    act.activation(hhi[:, k, :], mg[:, k, :], ACT.Copy).then_inc(m_hi.sem, 1)

            def outs(here, layer, e):
                for j in range(2):
                    act.wait_ge(*emptied[j].at(here, 0))
                    act.dma_start(S(8 + j), x_d[bass.ds(e * 2 + j, 1)].rearrange("k p t -> p (k t)")).then_inc(xo_in[j].sem, 16)

            layers(act, pro, head, nothing, branch, merge, join, outs)

            act.wait_ge(*last(x_ready))
            for k in range(KB):
                if k >= 2:
                    act.wait_ge(*once(fin, k - 1))
                act.activation(W[1 + k % 2], xs[:, k, :], ACT.Square).then_inc(sq.sem, 1)
            act.preload_act_table_set(LNEXP)
            act.wait_ge(*last(ssq, 1))
            act.activation(W[3], m01, ACT.Ln, bias=EPS, scale=1.0 / D).then_inc(fin_a.sem, 1)
            act.wait_ge(*once(fin_a, 1))
            act.activation(W[3], W[3], ACT.Exp, scale=-0.5).then_inc(rstd.sem, 1)
            for n in range(NT):
                act.wait_ge(*once(fin_t, n + 1))
                if n >= 2:
                    act.wait_ge(*once(y_out[n % 2], n // 2))
                act.activation(W[5 + n % 2], dense[n % 2], ACT.Copy).then_inc(fin_c.sem, 1)
                act.wait_ge(*once(fin_c, n + 1))
                act.dma_start(out[0, n * P:(n + 1) * P, :], W[5 + n % 2]).then_inc(y_out[n % 2].sem, 16)
            act.wait_ge(*once(y_out[0], 4))
            act.wait_ge(*once(y_out[1], 4))
            act.wait_ge(*last(a_stored))
            act.wait_ge(*last(b_st))
            act.wait_ge(*last(c_stored))

        @block.vector
        def _(dve):
            step = own["dve"]

            def counted(here):
                n = [0]

                def link(ins):
                    n[0] += 1
                    ins.then_inc(step.sem, 1)
                    dve.wait_ge(*step.at(here, n[0]))
                return n, link

            def tally(phase, n):
                assert n[0] == OWN["dve"][phase], (phase, n)

            def told(here, ins, ev, k):
                ins.then_inc(ev.sem, 1)
                dve.wait_ge(*ev.at(here, k))

            begin(dve, b_done, a_done, c_done, br_taken, u_lo)
            dve.wait_ge(*once(setup_t, 1))
            dve.tensor_copy(prm, m01[:, 0:R_END]).then_inc(setup_c.sem, 1)
            dve.tensor_copy(bmg, m01[:, 128:128 + DEPTH * 24]).then_inc(setup_c.sem, 1)
            dve.wait_ge(*once(setup_c, 2))
            dve.tensor_tensor(small[:, 0:4], prm[:, R_LB:R_LB + 4], prm[:, R_LB + 4:R_LB + 8], ALU.max).then_inc(setup_c.sem, 1)
            dve.wait_ge(*once(setup_c, 3))
            lb3 = prm[:, R_LB:R_LB + 8].rearrange("p (l h) -> p l h", l=2)
            mx3 = small[:, 0:4].unsqueeze(1).to_broadcast([P, 2, 4])
            dve.tensor_tensor(small[:, 16:24].rearrange("p (l h) -> p l h", l=2), lb3, mx3, ALU.subtract).then_inc(setup_c.sem, 1)
            dve.wait_ge(*once(setup_c, 5))
            e0, e1 = prm[:, R_LB:R_LB + 4], prm[:, R_LB + 4:R_LB + 8]
            k = [5]

            def then(ins):
                k[0] += 1
                ins.then_inc(setup_c.sem, 1)
                dve.wait_ge(*once(setup_c, k[0]))
            then(dve.tensor_tensor(small[:, 0:4], e0, e1, ALU.add))
            then(dve.reciprocal(small[:, 4:8], small[:, 0:4]))
            then(dve.tensor_tensor(small[:, 8:12], e0, small[:, 4:8], ALU.mult))
            then(dve.tensor_tensor(small[:, 12:16], e1, small[:, 4:8], ALU.mult))
            then(dve.tensor_tensor(small[:, 0:4], small[:, 8:12], small[:, 12:16], ALU.add))
            then(dve.tensor_tensor(e0, small[:, 8:12], small[:, 8:12], ALU.subtract))
            then(dve.tensor_tensor(e1, small[:, 0:4], small[:, 8:12], ALU.subtract))
            for h in range(2):
                r = slice(h * CHUNK, (h + 1) * CHUNK)
                then(dve.tensor_copy(sinks[r, :], sinks_all[r, :].rearrange("p (c h) -> p c h", h=2)[:, :, h]))
            for n in range(NT):
                dve.wait_ge(*once(x_t, n + 1))
                dve.tensor_copy(xs[:, :, n * P:(n + 1) * P], dense[n % 2].rearrange("p (k c) -> p k c", c=P)).then_inc(x_c.sem, 1)
            dve.wait_ge(*once(x_c, NT))
            dve.sem_inc(x_ready.sem, 1)

            def pro(here, layer):
                n, link = counted(here)
                plain(dve)
                link(dve.tensor_copy(ng, prm[:, bass.ds(layer * KB + R_NG, KB)]))
                for k in range(KB):
                    dve.wait_ge(*sq.at(here, k + 1))
                    if k == 0:
                        ins = dve.tensor_copy(W[0], W[1])
                    else:
                        ins = dve.tensor_tensor(W[0], W[0], W[1 + k % 2], ALU.add)
                    told(here, ins, sq_sum, k + 1)
                dve.wait_ge(*rstd.at(here, 1))
                for k in range(KB):
                    if k >= 2:
                        dve.wait_ge(*h_hi.at(here, k - 1))
                        dve.wait_ge(*h_lo.at(here, k - 1))
                    ins = dve.scalar_tensor_tensor(W[4 + k % 2], xs[:, k, :], ng[:, k:k + 1], W[3], ALU.mult, ALU.mult)
                    told(here, ins, hn, k + 1)
                    if k:
                        lo(here, k - 1)
                lo(here, KB - 1)
                for g in range(2):
                    dve.wait_ge(*k_rot.at(here, 2 * g + 1))
                    told(here, dve.tensor_tensor(kd[g], m01, cos, ALU.mult), k_cos, 2 * g + 1)
                    dve.wait_ge(*k_rot.at(here, 2 * g + 2))
                    told(here, dve.tensor_tensor(W[1], m23, sin, ALU.mult), k_cos, 2 * g + 2)
                    told(here, dve.tensor_tensor(kd[g], kd[g], W[1], ALU.add), kd_done, g + 1)
                dve.wait_ge(*block_done.at(here, 3))
                told(here, dve.tensor_scalar(W[3][0:8, :], dense[0][0:8, :], gb[0:8, bass.ds(layer, 1)], None, ALU.add), if_copied, 1)
                dve.sem_inc(emptied[0].sem, 1)
                dve.wait_ge(*f_moved.at(here, 1))
                f, lf, cum, m, a, ig, wend = W[4][0:4, :], W[6][0:4, :], W[1][0:4, :], W[7][0:4, :], W[8][0:4, :], W[3][0:4, :], W[5][0:4, :]
                link(dve.tensor_scalar(lf, f, 0.0, None, ALU.min))
                dve.wait_ge(*r_abs.at(here, 1))
                link(dve.tensor_tensor(lf, lf, wend, ALU.subtract))
                link(dve.tensor_tensor_scan(m, lf, ig, 0.0, ALU.add, ALU.max))
                for t in range(NT):
                    c = slice(t * P, (t + 1) * P)
                    link(dve.tensor_tensor_scan(cum[:, c], ones[0:4, :], lf[:, c], 0.0, ALU.mult, ALU.add))
                link(dve.tensor_tensor(a, cum, m, ALU.subtract))
                link(dve.tensor_tensor(ig, ig, cum, ALU.subtract))
                link(dve.tensor_tensor(tiles(wend), tiles(ig), tiles(a)[:, :, P - 1:P].to_broadcast([4, NT, P]), ALU.add))
                link(dve.tensor_copy(lf[:, 0:P], a[:, 0:P]))
                told(here, dve.tensor_tensor(tiles(lf)[:, 1:NT, :], tiles(a)[:, 1:NT, :],
                                             tiles(m)[:, 0:NT - 1, P - 1:P].to_broadcast([4, NT - 1, P]), ALU.add), r_sums, 1)
                dve.wait_ge(*r_inter.at(here, 1))
                told(here, dve.tensor_copy(small[0:4, 0:NT], tiles(lf)[:, :, P - 1]), r_dec, 1)
                dve.wait_ge(*r_t.at(here, 1))
                link(dve.tensor_copy(bcol, mb[2][:, 0:32]))
                told(here, dve.tensor_copy(wcol, mb[2][:, 32:64]), r_col, 1)
                tally("pro", n)

            def lo(here, k):
                dve.wait_ge(*h_hi.at(here, k + 1))
                dve.tensor_tensor(hlo[:, k, :], W[4 + k % 2], hhi[:, k, :].bitcast(F32), ALU.subtract).then_inc(h_lo.sem, 1)

            def head(here, layer, i, g):
                n, link = counted(here)
                dve.wait_ge(*c_done.at(here, 0))
                for w in range(4):
                    plain(dve)
                    link(dve.tensor_copy(hp[:, 2 * w:2 * w + 2], prm[:, bass.ds(layer * 32 + i + w * 8, 5)][:, 0:5:4]))
                plain(dve)
                link(dve.tensor_copy(hp[:, 8:10], prm[:, bass.ds(layer * 8 + i + R_CB, 5)][:, 0:5:4]))
                plain(dve)
                link(dve.tensor_copy(hp[:, 10:11], prm[:, bass.ds(layer * 4 + i + R_LB, 1)]))
                plain(dve)
                link(dve.tensor_copy(hp[:, 12:13], prm[:, bass.ds(layer + R_AG, 1)]))
                plain(dve)
                link(dve.tensor_copy(hp[:, 13:14], prm[:, bass.ds(layer * 4 + i + R_CG, 1)]))
                plain(dve)
                link(dve.tensor_copy(hp[:, 14:15], sinks[:, bass.ds(layer * 4 + i, 1)]))
                told(here, dve.tensor_scalar(hp[:, 11:12], hp[:, 10:11], -1.0, 1.0, ALU.mult, ALU.add), hp_done, 1)
                dve.wait_ge(*v_sh.at(("head", layer, 0), 0))
                plain(dve)
                link(dve.tensor_copy(W[6], slots[:, bass.ds(g + 19, 1), :].rearrange("p o t -> p (o t)")))
                for src, dst, m in ((vtok, W[4], NT), (vsh, W[5], NT - 1)):
                    for h in range(2):
                        v = src.rearrange("p (t g c) -> p g t c", g=2, c=CHUNK)[:, bass.ds(g, 1), 0:m, :].rearrange("p o t c -> p (o t) c")
                        plain(dve)
                        link(dve.tensor_copy(dst.rearrange("p (t g c) -> p t g c", g=2, c=CHUNK)[:, 0:m, h, :], v))
                dve.wait_ge(*b_rope.at(here, 1))
                link(dve.tensor_tensor(W[7], m01, sin, ALU.mult))
                link(dve.tensor_tensor(bq, bq, cos, ALU.mult))
                told(here, dve.tensor_tensor(bq, bq, W[7], ALU.add), b_qr, 1)
                sc_mx, sc_d, sc_e, sc_s, sc_r = (small[:, 16 * m:16 * m + 16] for m in range(5))
                for q in range(4):
                    c4 = slice(4 * q, 4 * q + 4)
                    dve.wait_ge(*b_s.at(here, q + 1))
                    if q == 0:
                        link(dve.memset(mb[0][:, CHUNK:P], NEG))
                    s3 = mb[q].rearrange("p (c k) -> p c k", k=P)
                    p3 = tiles(W[q // 2])[:, (q % 2) * 4:(q % 2) * 4 + 4, :]
                    link(dve.tensor_reduce(sc_mx[:, c4], s3, AX, ALU.max))
                    link(dve.tensor_scalar(sc_mx[:, c4], sc_mx[:, c4], SCALE_B, hp[:, 14:15], ALU.mult, ALU.max))
                    link(dve.tensor_scalar(sc_d[:, c4], sc_mx[:, c4], -1.0, hp[:, 14:15], ALU.mult, ALU.add))
                    told(here, dve.scalar_tensor_tensor(p3, s3, SCALE_B, sc_mx[:, c4].unsqueeze(2).to_broadcast([P, 4, P]), ALU.mult, ALU.subtract), b_d, q + 1)
                for q in range(4):
                    c4 = slice(4 * q, 4 * q + 4)
                    p3 = tiles(W[q // 2])[:, (q % 2) * 4:(q % 2) * 4 + 4, :]
                    dve.wait_ge(*b_e.at(here, q + 1))
                    link(dve.tensor_reduce(sc_s[:, c4], p3, AX, ALU.add))
                    dve.wait_ge(*own["act"].at(here, q + 1))
                    link(dve.tensor_tensor(sc_s[:, c4], sc_s[:, c4], sc_e[:, c4], ALU.add))
                    link(dve.reciprocal(sc_r[:, c4], sc_s[:, c4]))
                    told(here, dve.tensor_tensor(p3, p3, sc_r[:, c4].unsqueeze(2).to_broadcast([P, 4, P]), ALU.mult), b_p, q + 1)
                dve.wait_ge(*a_sig.at(here, 1))
                link(dve.tensor_scalar(ak, ak, hp[:, 11:12], hp[:, 10:11], ALU.mult, ALU.add))
                dve.wait_ge(*b_z.at(here, 1))
                dve.wait_ge(*c_stored.at(here, 0))
                for q in range(4):
                    dve.wait_ge(*b_o.at(here, q + 1))
                    for h in range(2):
                        r = slice(h * CHUNK, (h + 1) * CHUNK)
                        o3 = mb[q][r, :].rearrange("p (c k) -> p c k", k=P)[:, :, h * CHUNK:(h + 1) * CHUNK]
                        cc = slice(q * 256, (q + 1) * 256)
                        ins = dve.tensor_tensor(W[8][r, cc].rearrange("p (c k) -> p c k", k=CHUNK), o3,
                                                z0[r, cc].rearrange("p (c k) -> p c k", k=CHUNK), ALU.mult)
                        if (q, h) == (3, 1):
                            told(here, ins, b_done, 1)
                        else:
                            link(ins)
                told(here, dve.tensor_scalar(W[0], ak, TINY, None, ALU.max), a_f, 1)
                told(here, dve.tensor_scalar(ak, ak, -1.0, 1.0, ALU.mult, ALU.add), a_k, 1)
                dve.wait_ge(*a_ln.at(here, 1))
                for t in range(NT):
                    c = slice(t * P, (t + 1) * P)
                    ins = dve.tensor_tensor_scan(W[1][:, c], ones, W[0][:, c], 0.0, ALU.mult, ALU.add)
                    if t == NT - 1:
                        told(here, ins, a_cum, 1)
                    else:
                        link(ins)
                cum = W[1]

                def exponents(m):
                    kq = W[2 + m % 3]
                    if m >= 3:
                        dve.wait_ge(*a_lv.at(here, m - 2))
                    if m == 7:
                        told(here, dve.tensor_tensor(tiles(kq), tiles(cum)[:, :, P - 1:P].to_broadcast([P, NT, P]), tiles(cum), ALU.subtract), a_diff, 8)
                        return
                    h = 64 >> m
                    c3, k3 = (v.rearrange("p (b e) -> p b e", e=2 * h) for v in (cum, kq))
                    ref = c3[:, :, h - 1:h].to_broadcast([P, T // (2 * h), h])
                    link(dve.tensor_tensor(k3[:, :, h:2 * h], c3[:, :, h:2 * h], ref, ALU.subtract))
                    told(here, dve.tensor_tensor(k3[:, :, 0:h], ref, c3[:, :, 0:h], ALU.subtract), a_diff, m + 1)

                def decayed(m):
                    kq = W[2 + m % 3]
                    dve.wait_ge(*a_e.at(here, m + 1))
                    if m == 7:
                        told(here, dve.tensor_tensor(kq, kq, ak, ALU.mult), a_kq, 8)
                        return
                    h = 64 >> m
                    k3, q3, f3 = (v.rearrange("p (b e) -> p b e", e=2 * h) for v in (kq, aq, ak))
                    link(dve.scalar_tensor_tensor(k3[:, :, h:2 * h], q3[:, :, h:2 * h], SCALE, k3[:, :, h:2 * h], ALU.mult, ALU.mult))
                    told(here, dve.tensor_tensor(k3[:, :, 0:h], k3[:, :, 0:h], f3[:, :, 0:h], ALU.mult), a_kq, m + 1)

                def taken(m):
                    h = 64 >> m
                    dve.wait_ge(*a_lv.at(here, m + 1))
                    o = tiles(W[6]).rearrange("p t (b e) -> p t b e", e=2 * h)[:, :, :, h:2 * h]
                    mask = cst[:, C_LVL + 64 * m:C_LVL + 64 * m + 64].bitcast(I32).rearrange("p (b r) -> p b r", r=h)
                    mask = mask.unsqueeze(1).to_broadcast([P, NT, 64 // h, h])
                    data = mb[m % 2].rearrange("p (t b r) -> p t b r", t=NT, r=h)
                    plain(dve)
                    told(here, dve.copy_predicated(o, mask, data), a_pr, m + 1)

                def taps(j, ev, dst, col, out_ev):
                    dve.wait_ge(*ev.at(here, 1))
                    src = dense[j % 2]
                    for w in (2, 1, 0):
                        d = 3 - w
                        ins = dve.scalar_tensor_tensor(dst[:, d:T], src[:, 0:T - d], hp[:, 2 * w + col:2 * w + col + 1], dst[:, d:T], ALU.mult, ALU.add)
                        if w == 0 and out_ev is not None:
                            told(here, ins, out_ev, 1)
                        elif w == 0:
                            ins.then_inc(emptied[j % 2].sem, 1)
                            dve.wait_ge(*emptied[j % 2].at(here, j // 2 + 1))
                        else:
                            link(ins)
                    if out_ev is not None:
                        dve.sem_inc(emptied[j % 2].sem, 1)

                exponents(0)
                exponents(1)
                dve.wait_ge(*a_q.at(here, 1))
                decayed(0)
                exponents(2)
                decayed(1)
                decayed(2)
                dve.wait_ge(*a_dg.at(here, 1))
                for h in range(2):
                    idb = ident.unsqueeze(1).to_broadcast([P, 4, P])
                    told(here, dve.scalar_tensor_tensor(tiles(W[6])[:, 4 * h:4 * h + 4, :], tiles(m23)[:, 4 * h:4 * h + 4, :], SCALE, idb, ALU.mult, ALU.mult), a_sa, h + 1)
                taken(0)
                exponents(3)
                taps(5, c_qc, cq, 0, c_qt)
                taken(1)
                decayed(3)
                exponents(4)
                taken(2)
                decayed(4)
                for m in range(5, 8):
                    exponents(m)
                    taken(m - 2)
                    decayed(m)
                taken(6)
                dve.wait_ge(*a_e.at(here, 9))
                told(here, dve.scalar_tensor_tensor(W[5], aq, SCALE, W[5], ALU.mult, ALU.mult), a_kq, 9)
                el = small[:, 0:NT]
                told(here, dve.tensor_copy(el, tiles(cum)[:, :, P - 1]), a_last, 1)
                dve.wait_ge(*a_vt.at(here, 1))
                taps(6, c_kc, ck, 1, None)
                dve.wait_ge(*a_el.at(here, 1))
                dve.wait_ge(*a_u.at(here, 1))
                for t in range(1, NT):
                    c, before = slice(t * P, (t + 1) * P), slice((t - 1) * P, t * P)
                    if t == 1:
                        ins = dve.tensor_copy(ast[:, c], m01[:, before])
                    else:
                        ins = dve.scalar_tensor_tensor(ast[:, c], ast[:, before], small[:, 8 + t - 1:8 + t], m01[:, before], ALU.mult, ALU.add)
                    if t == NT - 1:
                        told(here, ins, a_st, 1)
                    else:
                        link(ins)
                dve.wait_ge(*c_in.at(here, 3))
                dve.wait_ge(*r_col.at(("head", layer, 0), 0))
                d3 = tiles(W[0])
                link(dve.tensor_tensor(d3, d3, negm.unsqueeze(1).to_broadcast([P, NT, P]), ALU.add))
                told(here, dve.tensor_tensor(d3, d3, bcol[:, bass.ds(i * NT, NT)].unsqueeze(2).to_broadcast([P, NT, P]), ALU.add), c_dx, 1)
                dve.wait_ge(*c_q.at(here, 1))
                told(here, dve.scalar_tensor_tensor(W[1], cq, SCALE, W[1], ALU.mult, ALU.mult), c_qp, 1)
                dve.wait_ge(*a_rs.at(here, 1))
                dve.wait_ge(*a_z.at(here, 1))
                dve.wait_ge(*b_st.at(here, 1))
                link(dve.scalar_tensor_tensor(W[8], W[4], hp[:, 12:13], W[3], ALU.mult, ALU.mult))
                told(here, dve.tensor_tensor(W[8], W[8], z0, ALU.mult), a_done, 1)
                dve.wait_ge(*c_kt.at(here, 1))
                for h in range(2):
                    wb = wcol[:, bass.ds(i * NT + 4 * h, 4)].unsqueeze(2).to_broadcast([P, 4, P])
                    told(here, dve.tensor_tensor(tiles(W[6])[:, 4 * h:4 * h + 4, :], tiles(m01)[:, 4 * h:4 * h + 4, :], wb, ALU.mult), c_kw, h + 1)
                dve.wait_ge(*c_dm.at(here, 1))
                dve.wait_ge(*c_s.at(here, 1))
                for h in range(2):
                    t = slice(h * HALF, (h + 1) * HALF)
                    told(here, dve.scalar_tensor_tensor(W[0][:, t], m23[:, t], SCALE, W[0][:, t], ALU.mult, ALU.mult), c_sc, h + 1)
                dve.wait_ge(*c_u.at(here, 1))
                link(dve.memset(nst[:, 0:1], 0.0))
                plain(dve)
                link(dve.tensor_copy(small[:, 0:NT], dec[:, bass.ds(i * NT, NT)]))
                for t in range(1, NT):
                    c, before = slice(t * P, (t + 1) * P), slice((t - 1) * P, t * P)
                    if t == 1:
                        link(dve.tensor_copy(nst[:, 1:2], m23[:, 0:1]))
                        ins = dve.tensor_copy(cst_v[:, c], m01[:, before])
                    else:
                        link(dve.scalar_tensor_tensor(nst[:, t:t + 1], nst[:, t - 1:t], small[:, t - 1:t], m23[:, 2 * t - 2:2 * t - 1], ALU.mult, ALU.add))
                        ins = dve.scalar_tensor_tensor(cst_v[:, c], cst_v[:, before], small[:, t - 1:t], m01[:, before], ALU.mult, ALU.add)
                    if t == NT - 1:
                        told(here, ins, c_st, 1)
                    else:
                        link(ins)
                link(dve.tensor_tensor(tiles(W[2]), tiles(W[1]), nst.unsqueeze(2).to_broadcast([P, NT, P]), ALU.mult))
                told(here, dve.tensor_tensor(W[2], W[2], W[0], ALU.add), c_t, 1)
                dve.wait_ge(*c_ab.at(here, 1))
                told(here, dve.tensor_tensor(W[3], W[3], W[7], ALU.max), c_mx, 1)
                dve.wait_ge(*c_r.at(here, 1))
                dve.wait_ge(*c_o.at(here, 1))
                dve.wait_ge(*a_stored.at(here, 1))
                told(here, dve.tensor_tensor(W[8], m23, W[3], ALU.mult), c_h, 1)
                dve.wait_ge(*c_rs.at(here, 1))
                link(dve.scalar_tensor_tensor(W[8], W[8], hp[:, 13:14], W[3], ALU.mult, ALU.mult))
                dve.wait_ge(*c_zo.at(here, 1))
                link(dve.tensor_tensor(W[8], W[8], z1, ALU.mult))
                dve.wait_ge(*c_zz.at(here, 1))
                told(here, dve.tensor_tensor(W[8], W[8], z2, ALU.mult), c_done, 1)
                tally("head", n)

            def mid(here, layer):
                dve.wait_ge(*c_stored.at(here, 0))
                dve.memset(slots[:, 12:20, :], 0.0).then_inc(cleared.sem, 1)
                dve.wait_ge(*cleared.at(("branch", layer, 0), 0))

            def branch(here, merging, b):
                for k in range(4):
                    dve.wait_ge(*u_hi.at(here, k + 1))
                    dve.tensor_tensor(ulo[:, k, :], us[:, k, :], uhi[:, k, :].bitcast(F32), ALU.subtract).then_inc(u_lo.sem, 1)

            def merge(here, layer, b, d):
                n, link = counted(here)
                for j in range(2):
                    dve.wait_ge(*g_sig.at(here, j + 1))
                    if j == 0:
                        dve.wait_ge(*br_done.at(here, 1))
                    else:
                        dve.wait_ge(*block_done.at(here, 3))
                    link(dve.tensor_tensor(gt, ga[j], (m01, m23)[j], ALU.mult))
                    dst = slots[:, bass.ds(d * 2 + (12 + j), 1), :].rearrange("p o t -> p (o t)")
                    told(here, dve.tensor_tensor(dst, dst, gt, ALU.add), br_taken, j + 1)
                tally("merge", n)

            def join(here, layer):
                for k in range(KB):
                    dve.wait_ge(*m_hi.at(here, k + 1))
                    dve.tensor_tensor(hlo[:, k, :], mg[:, k, :], hhi[:, k, :].bitcast(F32), ALU.subtract).then_inc(m_lo.sem, 1)

            def outs(here, layer, e):
                for j in range(2):
                    dve.wait_ge(*block_done.at(here, j + 1))
                    dve.wait_ge(*xo_in[j].at(here, 1))
                    dst = slots[:, bass.ds(e * 2 + j, 1), :].rearrange("p o t -> p (o t)")
                    told(here, dve.tensor_tensor(dst, dense[j], S(8 + j), ALU.add), x_ready, j + 1)
                    dve.sem_inc(emptied[j].sem, 1)

            layers(dve, pro, head, mid, branch, merge, join, outs, True)

            for k in range(KB):
                dve.wait_ge(*last(sq, k + 1))
                if k == 0:
                    ins = dve.tensor_copy(W[0], W[1])
                else:
                    ins = dve.tensor_tensor(W[0], W[0], W[1 + k % 2], ALU.add)
                ins.then_inc(fin.sem, 1)
                dve.wait_ge(*once(fin, k + 1))
            dve.wait_ge(*last(rstd, 1))
            for k in range(KB):
                dve.scalar_tensor_tensor(xs[:, k, :], xs[:, k, :], prm[:, R_FG + k:R_FG + k + 1], W[3], ALU.mult, ALU.mult).then_inc(fin.sem, 1)


_INS = ["x", "norm_g", "w_in", "conv_w", "conv_b", "hgrn_lb", "hgrn_norm_g", "attn_sinks", "mlstm_gate_b",
        "mlstm_norm_g", "w_mg", "b_mg", "w_br", "w_out", "final_g"]


def kernel(**inputs):
    import concourse.bacc as bacc
    from concourse.bass_utils import run_bass_kernel_spmd

    nc = bacc.Bacc("TRN2", target_bir_lowering=False, num_devices=1)
    table, dups = constants()
    arrays = {f"in_{n}": np.ascontiguousarray(inputs[n]) for n in _INS} | {"in_consts": table, "in_dups": dups}
    args = {n[3:]: nc.dram_tensor(n, a.shape, mybir.dt.from_np(a.dtype), kind="ExternalInput").ap() for n, a in arrays.items()}
    args["out"] = nc.dram_tensor("out_0", (1, T, D), F32, kind="ExternalOutput").ap()
    build(nc, **args)
    return run_bass_kernel_spmd(nc, [arrays], core_ids=[0]).results[0]["out_0"]
```

```python
from contextlib import ExitStack

import numpy as np

import concourse.bass as bass
from concourse import mybir

F32 = mybir.dt.float32
F32R = mybir.dt.float32r
I32 = mybir.dt.int32
ALU = mybir.AluOpType
ACT = mybir.ActivationFunctionType
AX = mybir.AxisListType.X

P = 128
DEPTH = 2
D = 1024
T = 1024
KB = D // P
NT = T // P
HALF = 512
HEADS = 4
BR = 512
CHUNK = 64
EPS = 1e-6
TINY = 1e-30
NEG = -1e30
SCALE = float(P) ** -0.5
SCALE_B = float(CHUNK) ** -0.5
THETA = 500000.0
LEVELS = 7

AQ, AF, AI, AZ, BQ, BK, BV, BZ = 0, 512, 1024, 1536, 2048, 2560, 2688, 2816
CQ, CK, CV, CIF, CO, CZ = 3328, 3840, 4352, 4864, 4872, 5384

RING = 3
BEHIND = (2, 2, 3)

C_ID, C_ONE, C_ROT, C_NEG, C_LVL = 0, 128, 256, 384, 512
C_COS = C_LVL + 64 * LEVELS
C_SIN = C_COS + T
C_END = C_SIN + T

R_CW, R_CB, R_LB, R_CG, R_AG, R_NG, R_FG, R_END = 0, 64, 80, 88, 96, 98, 114, 122

PHASES = {"pro": 1, "head0": 1, "head": 3, "tail": 1, "branch": 3, "merge": 12, "join": 1, "out": 4}
OWN = {"pool": {"pro": 3, "head0": 11, "head": 11, "merge": 3, "out": 2},
       "act": {"pro": 4, "head0": 5, "head": 7, "tail": 2},
       "dve": {"pro": 16, "head0": 83, "head": 101, "tail": 19, "merge": 2}}


class Event:

    def __init__(self, sem, first, per, by):
        self.sem, self.first, self.per, self.by = sem, first, per, by
        self.layer = sum(per.get(p, 0) * n for p, n in PHASES.items())

    def at(self, here, k):
        phase, layer, index = here
        before = 0
        for p, n in PHASES.items():
            if p == phase:
                break
            before += self.per.get(p, 0) * n
        assert self.first + before + k > 0, "a wait against a register's value stays positive"
        value = layer * (self.layer * self.by) + (self.first + before + k) * self.by
        if self.per.get(phase, 0) and not (isinstance(index, int) and index == 0):
            value = value + index * (self.per[phase] * self.by)
        return self.sem, value


def constants():
    c = np.zeros((P, C_END), np.float32)
    k = np.arange(P)
    c[:, C_ID:C_ID + P] = np.eye(P)
    c[:, C_ONE:C_ONE + P] = 1.0
    rot = np.zeros((P, P), np.float32)
    for m in range(P):
        r = m % CHUNK
        if r < 8:
            rot[m + 8, m] = -1.0
        elif r < 16:
            rot[m - 8, m] = 1.0
    c[:, C_ROT:C_ROT + P] = rot
    c[:, C_NEG:C_NEG + P] = np.where(k[:, None] > k[None, :], NEG, 0.0)
    for n in range(LEVELS):
        h = 64 >> n
        j = np.arange(64)
        block = j // h
        c[:, C_LVL + 64 * n:C_LVL + 64 * n + 64] = (k[:, None] // (2 * h) == block[None, :]) & (k[:, None] % (2 * h) < h)
    inv = np.float32(THETA) ** (-np.arange(8, dtype=np.float32) / 8)
    ang = np.arange(T, dtype=np.float32)[None, :] * inv[:, None]
    cos, sin = np.ones((P, T), np.float32), np.zeros((P, T), np.float32)
    for m in range(P):
        r = m % CHUNK
        if r < 16:
            cos[m], sin[m] = np.cos(ang[r % 8]), np.sin(ang[r % 8])
    c[:, C_COS:C_COS + T], c[:, C_SIN:C_SIN + T] = cos, sin
    dup = np.zeros((P, 4, P), np.float32)
    for g in range(2):
        for m in range(P):
            dup[CHUNK * g + m % CHUNK, g, m] = 1.0
        dup[:, 2 + g] = dup[:, g] @ rot
    return c, dup.reshape(P, 4 * P)


def tiles(ap):
    return ap.rearrange("p (t c) -> p t c", c=P)


def build(nc, x, norm_g, w_in, conv_w, conv_b, hgrn_lb, hgrn_norm_g, attn_sinks, mlstm_gate_b,
          mlstm_norm_g, w_mg, b_mg, w_br, w_out, final_g, consts, dups, out):
    ctx = ExitStack()
    with ctx:
        base = [-(-nc.sbuf_base // 64) * 64]

        def place(name, cols, dt=F32, at=None):
            t = nc.alloc_sbuf_tensor_at(name, [P, cols], dt, offset=base[0] if at is None else at)
            if at is None:
                base[0] += -(-cols // 8) * 32
            return t[:, :]

        raw = [place(f"w_raw{s}", D) for s in range(RING)]
        whi = [place(f"w_hi{s}", D, F32R) for s in range(RING)]
        wlo = [place(f"w_lo{s}", D, F32R) for s in range(RING)]
        hhi = place("h_hi", KB * T, F32R).rearrange("p (k t) -> p k t", k=KB)
        hlo = place("h_lo", KB * T, F32R).rearrange("p (k t) -> p k t", k=KB)
        slots_at = base[0]
        slots = place("slots", 23 * T).rearrange("p (s t) -> p s t", t=T)
        uhi = place("u_hi", 4 * T, F32R, slots_at + 4 * T * 4).rearrange("p (k t) -> p k t", k=4)
        ulo = place("u_lo", 4 * T, F32R, slots_at).rearrange("p (k t) -> p k t", k=4)
        cst = place("constant_table", C_END)
        prm = place("parameter_columns", R_END)
        bmg = place("b_mg_columns", DEPTH * 24)
        hp = place("head_parameters", 16)
        ng = place("norm_g_columns", KB)
        sinks_all = place("sinks_everywhere", 16)
        sinks = place("sink_columns", 8)
        bcol = place("b_columns", 32)
        wcol = place("w_end_columns", 32)
        dec = place("decays", 32)
        nst = place("n_states", NT)
        small = place("small", 16 * 5)
        gb = place("gate_bias", 2)
        assert base[0] <= nc.sbuf_usable_end, base[0] - nc.sbuf_usable_end

        ident = cst[:, C_ID:C_ID + P]
        ones = cst[:, C_ONE:C_ONE + P]
        rotm = cst[:, C_ROT:C_ROT + P]
        negm = cst[:, C_NEG:C_NEG + P]
        cos, sin = cst[:, C_COS:C_COS + T], cst[:, C_SIN:C_SIN + T]

        def S(n):
            return slots[:, n, :]

        aq, ak, avt, cq, ck, cvt, bq, z0, z1, z2 = (S(n) for n in range(10))
        ast, cst_v = avt, cvt
        W = [S(10 + n) for n in range(9)]
        kd = [S(19), S(20)]
        vtok, vsh = S(21), S(22)
        xs = slots[:, 0:8, :]
        us = slots[:, 0:4, :]
        mg = slots[:, 12:20, :]
        KQ = [cvt, W[7], W[2], W[3], W[4], W[5], W[2], W[3]]
        LEVEL_BANK = (0, 1, 2, 3, 0, 1, 0)
        ga = [S(20), S(21)]
        gt = S(22)
        U_ORDER = (0, 2, 3, 1)
        landing = [W[1], W[2], W[3], W[4], S(19), S(20), S(21), S(22)]

        psum = ctx.enter_context(nc.psum_tensor("psum", [P, 8 * HALF], F32))
        dense = [psum[:, 0:T], psum[:, T:2 * T]]
        mb = [psum[:, 2 * T + n * HALF:2 * T + (n + 1) * HALF] for n in range(4)]
        m01, m23 = psum[:, 2 * T:3 * T], psum[:, 3 * T:4 * T]

        x_d = nc.dram_tensor("x_feature_major", [KB, P, T], F32, kind="Internal").ap()
        u_d = nc.dram_tensor("branch_outputs", [3, HEADS, P, T], F32, kind="Internal").ap()
        row_d = nc.dram_tensor("gate_rows", [5, HEADS, T], F32, kind="Internal").ap()
        dec_d = nc.dram_tensor("decay_rows", [1, HEADS * NT], F32, kind="Internal").ap()

        def event(name, first=0, by=1, late=0, **per):
            if "head" in per:
                per.setdefault("head0", per["head"])
            if late:
                per["head"] = per["tail"] = late
            return Event(ctx.enter_context(nc.semaphore(name)), first, per, by)

        landed = [event(f"w_landed{s}", by=16, pro=1, head=(4, 4, 3)[s], merge=1, out=(1, 1, 0)[s]) for s in range(RING)]
        split = event("w_split", first=2, pro=3, head=11, merge=3, out=2)
        block_done = event("block_done", first=2, pro=3, head=11, merge=3, out=2)
        emptied = [event("dense0_emptied", first=1, pro=2, head=6, merge=1, out=1),
                   event("dense1_emptied", first=1, pro=2, head=5, merge=1, out=1)]
        ident_in = event("identity_landed", by=16)
        setup_in = event("setup_landed", by=16)
        table_in = event("tables_landed", by=16)
        setup_t = event("setup_transposed")
        setup_c = event("setup_copied")
        x_in = [event(f"x_landed{n}", by=16) for n in range(NT)]
        x_t = event("x_transposed")
        x_c = event("x_copied")
        x_ready = event("x_ready", first=1, out=2)
        sq = event("squared", first=NT, out=2)
        sum_cleared = event("sum_cleared", join=1)
        sq_sum = event("squares_summed", first=NT, out=2)
        ssq = event("sum_broadcast", pro=1)
        rstd = event("rstd_ready", pro=1)
        hn = event("h_normalised", pro=8)
        h_hi = event("h_hi_ready", pro=8)
        h_lo = [event("h_lo_even_ready", pro=4), event("h_lo_odd_ready", pro=4)]
        dup_in = event("dups_landed", by=16, pro=1)
        k_copied = event("k_copied", pro=1)
        k_rot = event("k_duplicated", pro=4)
        k_cos = event("k_duplicate_read", pro=4)
        kd_done = event("keys_ready", pro=2)
        v_copied = event("v_copied", pro=1)
        v_t = event("v_transposed", pro=1)
        v_tok = event("v_by_token", pro=1)
        v_sh = event("v_shifted", first=1, by=16, pro=2)
        if_copied = event("gate_rows_copied", pro=1)
        f_moved = event("f_rows_moved", by=16, pro=1)
        r_abs = event("f_abs", pro=1)
        r_scan = event("rows_scanned", pro=1)
        r_sums = event("row_sums_ready", pro=1)
        r_inter = event("inter_rows", pro=1)
        r_dec = event("decay_rows_ready", pro=1)
        r_exp = event("rows_ready", pro=1)
        r_out = event("rows_stored", by=16, pro=6)
        r_in = event("rows_reloaded", by=16, pro=3)
        r_t = event("row_columns_transposed", head0=1)
        r_col = event("row_columns_ready", head0=1)
        hp_done = event("head_parameters_ready", head=1)
        b_q = event("b_q_copied", head=1)
        b_z = event("b_gate", head=1)
        b_rope = event("b_q_rotated", head=1)
        b_qr = event("b_q_ready", head=1)
        b_s = event("b_scores", head=4)
        b_d = event("b_shifted", head=4)
        b_e = event("b_exp", head=4)
        b_p = event("b_probs", head=4)
        b_pt = event("b_probs_transposed", head=4)
        b_ptc = event("b_probs_copied", head=4)
        b_o = event("b_out", head=4)
        b_done = event("b_done", first=1, head=1)
        b_st = event("b_stored", first=1, by=16, head=1)
        a_q = event("a_q", head=1)
        a_sig = event("a_sigmoid", head=1)
        a_f = event("a_f", head=1)
        a_ln = event("a_log_f", head=1)
        a_v = event("a_v_copied", head=1)
        a_vt = event("a_v_transposed", head=1)
        a_vtok = event("a_v_by_token", head=1)
        a_k = event("a_k", head=1)
        a_cum = event("a_cum", head=1)
        a_diff = event("a_decay_exponents", head=8)
        a_e = event("a_decays", head=8)
        a_start = event("a_decays_from_start", head=1)
        a_kq = event("a_decayed", head=9)
        a_dg = event("a_diagonal", head=1)
        a_sa = event("a_diagonal_taken", head=2)
        a_lv = event("a_level", head=7)
        a_pr = event("a_level_taken", head=7)
        a_kt = event("a_k_transposed", head=1)
        a_ktc = event("a_k_by_token", head=1)
        a_u = event("a_updates", head=1)
        a_last = event("a_tile_exponents", head=1)
        a_el = event("a_tile_decays", head=1)
        a_st = event("a_states", head=1)
        a_o = event("a_out", head=1)
        a_oc = event("a_out_copied", head=1)
        a_sq = event("a_squared", head=1)
        a_ss = event("a_sum", head=1)
        a_rs = event("a_rstd", head=1)
        a_z = event("a_gate", head=1)
        a_done = event("a_done", first=1, head=1)
        a_stored = event("a_stored", first=1, by=16, head=1)
        c_qc = event("c_q_bias", head=1)
        c_kc = event("c_k_bias", head=1)
        c_qt = event("c_q_convolved", head=1)
        c_q = event("c_q", head=1)
        c_k = event("c_k", head=1)
        c_v = event("c_v_copied", head=1)
        c_in = event("c_rows_landed", by=16, head=3)
        c_vt = event("c_v_transposed", head=1)
        c_vtok = event("c_v_by_token", head=1)
        c_kt = event("c_k_transposed", head=1)
        c_kw = event("c_k_weighted", head=2)
        c_dx = event("c_dmat_exponents", head=1)
        c_dm = event("c_dmat", head=1)
        c_s = event("c_scores", head=1)
        c_sc = event("c_scores_weighted", head=2)
        c_qp = event("c_q_inter", head=1)
        c_u = event("c_updates", late=1)
        c_st = event("c_states", late=1)
        c_t = event("c_den_terms", late=1)
        c_o = event("c_num", late=1)
        c_den = event("c_den", late=1)
        c_ab = event("c_den_abs", late=1)
        c_mx = event("c_den_bounded", late=1)
        c_r = event("c_den_reciprocal", late=1)
        c_h = event("c_h", late=1)
        c_sq = event("c_squared", late=1)
        c_ss = event("c_sum", late=1)
        c_rs = event("c_rstd", late=1)
        c_zo = event("c_output_gate", head=1)
        c_zz = event("c_gate", head=1)
        c_done = event("c_done", first=1, late=1)
        c_stored = event("c_stored", first=1, by=16, late=1)
        u_in = event("u_landed", by=16, branch=1)
        u_hi = event("u_hi_ready", branch=4)
        u_lo = event("u_lo_ready", first=1, branch=4)
        g_sig = event("g_sigmoid", merge=2)
        br_done = event("branch_products", merge=1)
        br_taken = event("branch_taken", first=1, merge=2)
        m_hi = event("merged_hi", join=KB)
        m_lo = event("merged_lo", join=KB)
        xo_in = [event("x_old_landed0", by=16, out=1), event("x_old_landed1", by=16, out=1)]
        x_dst = event("x_stored", by=16, pro=1)
        fin = event("final_step")
        fin_t = event("final_transposed")
        fin_c = event("final_copied")
        fin_g = event("final_g_landed", by=16)
        y_out = [event(f"y_stored{n}", by=16) for n in range(4)]
        passed = ctx.enter_context(nc.semaphore("waits_passed"))
        own = {}
        for name, per in OWN.items():
            own[name] = event(name + "_step", **per)

        block = ctx.enter_context(nc.Block())

        def once(ev, k):
            return ev.sem, (ev.first + k) * ev.by

        def early(ev, k):
            return ev.sem, k * ev.by

        def last(ev, k=0):
            return ev.sem, (ev.first + DEPTH * ev.layer + k) * ev.by

        def begin(eng, *events):
            for ev in events:
                eng.sem_inc(ev.sem, ev.first * ev.by)

        def plain(eng):
            eng.sem_inc(passed, 1)

        def layers(eng, pro, head, tail, branch, merge, join, outs, calm=False):
            with eng.Fori(0, DEPTH, 1) as layer:
                pro(("pro", layer, 0), layer)
                if calm:
                    plain(eng)
                head(("head0", layer, 0), layer, 0, 0, False)
                if calm:
                    plain(eng)
                with eng.Fori(0, HEADS - 1, 1) as e:
                    head(("head", layer, e), layer, e + 1, (e + 1) // 2, True)
                tail(("tail", layer, 0), layer)
                if calm:
                    plain(eng)
                merge(("merge", layer, 0), layer, 0, 0)
                if calm:
                    plain(eng)
                with eng.Fori(0, 3, 1) as e:
                    merge(("merge", layer, e + 1), layer, 0, e + 1)
                with eng.Fori(0, 2, 1) as e:
                    b = e + 1
                    branch(("branch", layer, b), ("merge", layer, b * 4), b)
                    if calm:
                        plain(eng)
                    with eng.Fori(0, 4, 1) as d:
                        merge(("merge", layer, b * 4 + d), layer, b, d)
                join(("join", layer, 0), layer)
                if calm:
                    plain(eng)
                with eng.Fori(0, 4, 1) as e:
                    outs(("out", layer, e), layer, e)

        def wait_lo(eng, here, k):
            eng.wait_ge(*h_lo[k % 2].at(here, k // 2 + 1))

        def nothing(*_):
            pass

        @block.sync
        def _(sp):
            def load(here, j, src):
                sp.wait_ge(*split.at(here, j - BEHIND[min(j, 2)] + 1))
                plain(sp)
                s = j % RING
                sp.dma_start(raw[s].rearrange("p (k n) -> p k n", k=src.shape[1]), src).then_inc(landed[s].sem, 16)

            def cols(w, layer, c0, n=P):
                return w[bass.ds(layer, 1), :, bass.ds(c0, n)].rearrange("l (k p) n -> p (l k) n", p=P)

            for n in range(NT):
                sp.dma_start(landing[n], x[0, n * P:(n + 1) * P, :]).then_inc(x_in[n].sem, 16)
            rows = W[8]
            loads = [
                (rows[R_CW:R_CW + 64, 0:P], conv_w.rearrange("l w (j c) -> (l w j) c", c=P)),
                (rows[R_CB:R_CB + 16, 0:P], conv_b.rearrange("l (j c) -> (l j) c", c=P)),
                (rows[R_LB:R_LB + 8, 0:P], hgrn_lb.rearrange("l (j c) -> (l j) c", c=P)),
                (rows[R_CG:R_CG + 8, 0:P], mlstm_norm_g.rearrange("l (j c) -> (l j) c", c=P)),
                (rows[R_AG:R_AG + 2, 0:P], hgrn_norm_g),
                (rows[R_NG:R_NG + 16, 0:P], norm_g.rearrange("l (j c) -> (l j) c", c=P)),
                (rows[R_FG:R_FG + 8, 0:P], final_g.rearrange("(j c) -> j c", c=P)),
                (rows[0:DEPTH * 24, P:2 * P], b_mg.rearrange("l (j c) -> (l j) c", c=P)),
                (sinks_all, attn_sinks.rearrange("(o l) h -> o (l h)", o=1).partition_broadcast(P)),
                (gb[0:8, 0:1], mlstm_gate_b[0:1, :].rearrange("l h -> h l")),
                (gb[0:8, 1:2], mlstm_gate_b[1:2, :].rearrange("l h -> h l")),
            ]
            for dst, src in loads:
                sp.dma_start(dst, src).then_inc(setup_in.sem, 16)
            sp.dma_start(cst[:, 2 * P:C_END], consts[:, 2 * P:C_END]).then_inc(table_in.sem, 16)

            def pro(here, layer):
                for j, c0 in enumerate((CIF, BK, BV)):
                    load(here, j, cols(w_in, layer, c0))

            def head(here, layer, i, g, late):
                for j, c0 in enumerate((BQ, BZ, AF, AQ, CQ, AI, CK, CV, AZ, CO, CZ)):
                    load(here, j, cols(w_in, layer, i * P + c0))

            def merge(here, layer, b, d):
                for j in range(2):
                    load(here, j, cols(w_mg, layer, b * D + d * 256 + j * P))
                src = w_br[bass.ds(layer, 1), bass.ds(b, 1), :, bass.ds(d * 256, 256)]
                load(here, 2, src.rearrange("l b (k p) n -> p (l b k) n", p=P))

            def outs(here, layer, e):
                for j in range(2):
                    load(here, j, cols(w_out, layer, e * 256 + j * P))

            layers(sp, pro, head, nothing, nothing, merge, nothing, outs)

            sp.wait_ge(*m_lo.at(("join", DEPTH - 1, 0), KB))
            sp.dma_start(mg[:, 0, :], final_g.rearrange("(o c) -> o c", o=1).partition_broadcast(P)).then_inc(fin_g.sem, 16)
            for n in range(NT):
                sp.wait_ge(*once(fin_c, n + 1))
                sp.dma_start(out[0, n * P:(n + 1) * P, :], W[4 + n % 4]).then_inc(y_out[n % 4].sem, 16)
            for n in range(4):
                sp.wait_ge(*once(y_out[n], 2))

        @block.gpsimd
        def _(pool):
            begin(pool, split)
            step = own["pool"]

            def halve(here, j):
                s = j % RING
                pool.wait_ge(*landed[s].at(here, j // RING + 1))
                pool.wait_ge(*block_done.at(here, j - BEHIND[min(j, 2)] + 1))
                plain(pool)
                pool.tensor_copy(whi[s], raw[s]).then_inc(step.sem, 1)
                pool.wait_ge(*step.at(here, j + 1))
                pool.tensor_tensor(wlo[s], raw[s], whi[s].bitcast(F32), ALU.subtract).then_inc(split.sem, 1)

            def body(n):
                def run(here, *rest):
                    for j in range(n):
                        halve(here, j)
                return run

            def pro(here, layer):
                halve(here, 0)
                halve(here, 1)
                for k in range(1, KB, 2):
                    pool.wait_ge(*h_hi.at(here, k + 1))
                    plain(pool)
                    pool.tensor_tensor(hlo[:, k, :], W[4 + k % 4], hhi[:, k, :].bitcast(F32), ALU.subtract).then_inc(h_lo[1].sem, 1)
                halve(here, 2)

            layers(pool, pro, body(11), nothing, nothing, body(3), nothing, body(2))

        @block.tensor
        def _(pe):
            def transposes(src, dst, n0=0, n1=NT):
                for n in range(n0, n1):
                    ins = pe.transpose(dst[:, (n - n0) * P:(n - n0 + 1) * P], src[:, n * P:(n + 1) * P], ident)
                return ins

            def project(here, j, kk, hi, lo, dst, w0=0, step=P):
                s = j % RING
                for half in range(2):
                    t = slice(half * HALF, (half + 1) * HALF)
                    n = 0
                    for k in range(kk):
                        w = slice(k * step + w0, k * step + w0 + P)
                        for ww, xx in ((whi[s], hi), (wlo[s], hi), (whi[s], lo)):
                            ins = pe.matmul(dst[:, t], ww[:, w], xx[:, k, t], start=(n == 0), stop=(n == 3 * kk - 1))
                            n += 1
                return ins

            def project_landing(j, dst, ready):
                s = j % RING
                for k in range(KB):
                    ready(k)
                    w = slice(k * P, (k + 1) * P)
                    for half in range(2):
                        t = slice(half * HALF, (half + 1) * HALF)
                        for n, (ww, xx) in enumerate(((whi[s], hhi), (wlo[s], hhi), (whi[s], hlo))):
                            ins = pe.matmul(dst[:, t], ww[:, w], xx[:, k, t], start=(k == 0 and n == 0), stop=(k == KB - 1 and n == 2))
                return ins

            def wait_block(here, j, d, k):
                pe.wait_ge(*split.at(here, j + 1))
                pe.wait_ge(*emptied[d].at(here, k))

            begin(pe, block_done)
            pe.wait_ge(*once(ident_in, 1))
            for n in range(NT):
                pe.wait_ge(*once(x_in[n], 1))
                if n >= 2:
                    pe.wait_ge(*once(x_c, n - 1))
                dst = dense[n % 2]
                src = landing[n]
                for k in range(KB):
                    ins = pe.transpose(dst[:, k * P:(k + 1) * P], src[:, k * P:(k + 1) * P], ident)
                ins.then_inc(x_t.sem, 1)
            pe.wait_ge(*once(setup_in, 11))
            pe.transpose(m23[:, 0:R_END], W[8][0:R_END, 0:P], ident[0:R_END, 0:R_END])
            pe.transpose(m23[:, 128:128 + DEPTH * 24], W[8][0:DEPTH * 24, P:2 * P], ident[0:DEPTH * 24, 0:DEPTH * 24]).then_inc(setup_t.sem, 1)
            pe.wait_ge(*once(x_c, NT))

            def pro(here, layer):
                def duplicate(g, r):
                    dst = (m01, m23)[r]
                    for half in range(2):
                        ins = pe.matmul(dst[:, half * HALF:(half + 1) * HALF], z2[:, (2 * r + g) * P:(2 * r + g + 1) * P],
                                        W[0][:, half * HALF:(half + 1) * HALF], start=True, stop=True)
                    ins.then_inc(k_rot.sem, 1)

                pe.wait_ge(*sq_sum.at(here, 0))
                for half in range(2):
                    ins = pe.matmul(m01[:, half * HALF:(half + 1) * HALF], ones, W[0][:, half * HALF:(half + 1) * HALF], start=True, stop=True)
                ins.then_inc(ssq.sem, 1)
                wait_block(here, 0, 0, 0)
                project_landing(0, dense[0], lambda k: wait_lo(pe, here, k)).then_inc(block_done.sem, 1)
                wait_block(here, 1, 1, 0)
                project(here, 1, KB, hhi, hlo, dense[1]).then_inc(block_done.sem, 1)
                wait_block(here, 2, 0, 1)
                project(here, 2, KB, hhi, hlo, dense[0]).then_inc(block_done.sem, 1)
                pe.wait_ge(*k_copied.at(here, 1))
                pe.wait_ge(*dup_in.at(here, 1))
                duplicate(0, 0)
                duplicate(0, 1)
                pe.wait_ge(*v_copied.at(here, 1))
                pe.wait_ge(*emptied[1].at(here, 1))
                transposes(W[2], dense[1]).then_inc(v_t.sem, 1)
                for r in range(2):
                    pe.wait_ge(*k_cos.at(here, r + 1))
                    duplicate(1, r)

            def late_updates(here):
                pe.wait_ge(*a_rs.at(here, 0))
                pe.wait_ge(*c_kw.at(here, 0))
                pe.wait_ge(*c_sc.at(here, 0))
                for t in range(NT - 1):
                    c = slice(t * P, (t + 1) * P)
                    pe.matmul(m23[:, c], W[1][:, c], W[5][:, c], start=True, stop=True)
                    ins = pe.matmul(m01[:, 2 * t:2 * t + 2], W[1][:, c], ones[:, 0:2], start=True, stop=True)
                ins.then_inc(c_u.sem, 1)

            def late_outputs(here):
                pe.wait_ge(*c_st.at(here, 1))
                pe.wait_ge(*c_t.at(here, 1))
                for half in range(2):
                    t = slice(half * HALF, (half + 1) * HALF)
                    ins = pe.matmul(m01[:, t], ones, W[2][:, t], start=True, stop=True)
                ins.then_inc(c_den.sem, 1)
                for t in range(NT):
                    c = slice(t * P, (t + 1) * P)
                    ins = pe.matmul(m23[:, c], W[5][:, c], W[0][:, c], start=True, stop=(t == 0))
                    if t:
                        ins = pe.matmul(m23[:, c], cst_v[:, c], W[6][:, c], start=False, stop=True)
                ins.then_inc(c_o.sem, 1)

            def late_sum(here):
                pe.wait_ge(*c_sq.at(here, 1))
                for half in range(2):
                    t = slice(half * HALF, (half + 1) * HALF)
                    ins = pe.matmul(m01[:, t], ones, W[4][:, t], start=True, stop=True)
                ins.then_inc(c_ss.sem, 1)

            def gate_block(here, j):
                wait_block(here, j, j, 0)
                project(here, j, KB, hhi, hlo, dense[j]).then_inc(block_done.sem, 1)

            def tail(here, layer):
                gates = ("merge", layer, 0)
                gate_block(gates, 0)
                late_updates(here)
                gate_block(gates, 1)
                late_outputs(here)
                late_sum(here)
                pe.wait_ge(*c_rs.at(here, 1))

            def head(here, layer, i, g, late):
                def dense_block(j):
                    wait_block(here, j, j % 2, j // 2)
                    project(here, j, KB, hhi, hlo, dense[j % 2]).then_inc(block_done.sem, 1)

                def level(n):
                    h = 64 >> n
                    if n < 2:
                        pe.wait_ge(*a_vtok.at(here, 1))
                    elif n < 4:
                        pe.wait_ge(*a_sa.at(here, n - 1))
                    else:
                        pe.wait_ge(*a_pr.at(here, n - 3 if n < 6 else 5))
                    pe.wait_ge(*a_kq.at(here, n + 1))
                    for t in range(NT):
                        tile = KQ[n][:, t * P:(t + 1) * P]
                        ins = pe.matmul(mb[LEVEL_BANK[n]][:, t * 64:(t + 1) * 64], tile,
                                        tile.rearrange("p (b e) -> p b e", e=2 * h)[:, :, h:2 * h], start=True, stop=True)
                    ins.then_inc(a_lv.sem, 1)

                dense_block(0)
                if late:
                    late_updates(here)
                else:
                    pe.wait_ge(*r_in.at(("pro", layer, 0), 3))
                    pe.wait_ge(*k_cos.at(("pro", layer, 0), 4))
                    plain(pe)
                    pe.transpose(mb[2][:, 0:32], W[5][0:32, 0:P], ident[0:32, 0:32])
                    pe.transpose(mb[2][:, 32:64], W[5][0:32, P:2 * P], ident[0:32, 0:32]).then_inc(r_t.sem, 1)
                dense_block(1)
                if late:
                    late_outputs(here)
                dense_block(2)
                if late:
                    late_sum(here)
                else:
                    pe.wait_ge(*r_col.at(here, 1))
                pe.wait_ge(*b_q.at(here, 1))
                for half in range(2):
                    t = slice(half * HALF, (half + 1) * HALF)
                    ins = pe.matmul(m23[:, t], rotm, bq[:, t], start=True, stop=True)
                ins.then_inc(b_rope.sem, 1)
                dense_block(3)
                pe.wait_ge(*b_qr.at(here, 1))
                if late:
                    pe.wait_ge(*c_rs.at(here, 1))
                plain(pe)
                for q in range(4):
                    for c in range(4):
                        n = 4 * q + c
                        k0 = CHUNK * max(n - 1, 0)
                        for h in range(2):
                            r = slice(h * CHUNK, (h + 1) * CHUNK)
                            ins = pe.matmul(mb[q][r, c * P:(c + 1) * P], bq[r, n * CHUNK:(n + 1) * CHUNK],
                                            W[6][r, k0:k0 + P], start=True, stop=True)
                    ins.then_inc(b_s.sem, 1)
                def probs_transposed(q):
                    pe.wait_ge(*b_p.at(here, q + 1))
                    transposes(W[q // 2], mb[q], (q % 2) * 4, (q % 2) * 4 + 4).then_inc(b_pt.sem, 1)

                dense_block(4)
                for q in range(3):
                    probs_transposed(q)
                dense_block(5)
                probs_transposed(3)
                for q in range(4):
                    pe.wait_ge(*b_ptc.at(here, q + 1))
                    for c in range(4):
                        n = 4 * q + c
                        if n == 0:
                            v = W[4][:, 0:P]
                        elif n % 2:
                            v = W[4][:, (n // 2) * P:(n // 2 + 1) * P]
                        else:
                            v = W[5][:, (n // 2 - 1) * P:(n // 2) * P]
                        ins = pe.matmul(mb[q][:, c * P:(c + 1) * P], v, W[2 + q // 2][:, (n % 8) * P:(n % 8 + 1) * P], start=True, stop=True)
                    ins.then_inc(b_o.sem, 1)
                dense_block(6)
                pe.wait_ge(*a_v.at(here, 1))
                pe.wait_ge(*b_done.at(here, 1))
                transposes(avt, m01).then_inc(a_vt.sem, 1)
                pe.wait_ge(*a_k.at(here, 1))
                for t in range(NT):
                    c = slice(t * P, (t + 1) * P)
                    ins = pe.matmul(m23[:, c], ak[:, c], aq[:, c], start=True, stop=True)
                ins.then_inc(a_dg.sem, 1)
                for n in range(4):
                    level(n)
                dense_block(7)
                for n in range(4, 7):
                    level(n)
                pe.wait_ge(*a_kq.at(here, 8))
                transposes(KQ[7], m23).then_inc(a_kt.sem, 1)
                dense_block(8)
                pe.wait_ge(*a_ktc.at(here, 1))
                pe.wait_ge(*a_pr.at(here, 7))
                for t in range(NT - 1):
                    c = slice(t * P, (t + 1) * P)
                    ins = pe.matmul(m01[:, c], W[7][:, c], W[0][:, c], start=True, stop=True)
                ins.then_inc(a_u.sem, 1)
                pe.wait_ge(*c_v.at(here, 1))
                transposes(cvt, m23).then_inc(c_vt.sem, 1)
                dense_block(9)
                pe.wait_ge(*a_st.at(here, 1))
                pe.wait_ge(*a_kq.at(here, 9))
                pe.wait_ge(*c_vtok.at(here, 1))
                for t in range(NT):
                    c = slice(t * P, (t + 1) * P)
                    ins = pe.matmul(m23[:, c], W[0][:, c], W[6][:, c], start=True, stop=(t == 0))
                    if t:
                        ins = pe.matmul(m23[:, c], ast[:, c], W[1][:, c], start=False, stop=True)
                ins.then_inc(a_o.sem, 1)
                pe.wait_ge(*c_k.at(here, 1))
                transposes(ck, m01).then_inc(c_kt.sem, 1)
                dense_block(10)
                pe.wait_ge(*a_sq.at(here, 1))
                for half in range(2):
                    t = slice(half * HALF, (half + 1) * HALF)
                    ins = pe.matmul(m23[:, t], ones, W[2][:, t], start=True, stop=True)
                ins.then_inc(a_ss.sem, 1)
                pe.wait_ge(*c_kw.at(here, 2))
                pe.wait_ge(*c_q.at(here, 1))
                for t in range(NT):
                    c = slice(t * P, (t + 1) * P)
                    ins = pe.matmul(m01[:, c], ck[:, c], cq[:, c], start=True, stop=True)
                ins.then_inc(c_s.sem, 1)

            def merge(here, layer, b, d):
                if not (isinstance(b, int) and isinstance(d, int)):
                    gate_block(here, 0)
                    gate_block(here, 1)
                pe.wait_ge(*split.at(here, 3))
                pe.wait_ge(*u_lo.at(("branch", layer, b), 4))
                pe.wait_ge(*br_taken.at(here, 0))
                project(here, 2, 4, uhi, ulo, m01, 0, 256).then_inc(br_done.sem, 1)
                project(here, 2, 4, uhi, ulo, m23, P, 256).then_inc(block_done.sem, 1)

            def outs(here, layer, e):
                wait_block(here, 0, 0, 0)
                joined = ("join", layer, 0)
                for k in range(KB):
                    pe.wait_ge(*m_hi.at(joined, k + 1))
                    for half in range(2):
                        t = slice(half * HALF, (half + 1) * HALF)
                        for n, w in enumerate((whi[0], wlo[0])):
                            pe.matmul(dense[0][:, t], w[:, k * P:(k + 1) * P], hhi[:, k, t], start=(k == 0 and n == 0), stop=False)
                for k in range(KB):
                    pe.wait_ge(*m_lo.at(joined, k + 1))
                    for half in range(2):
                        t = slice(half * HALF, (half + 1) * HALF)
                        ins = pe.matmul(dense[0][:, t], whi[0][:, k * P:(k + 1) * P], hlo[:, k, t], start=False, stop=(k == KB - 1))
                ins.then_inc(block_done.sem, 1)
                wait_block(here, 1, 1, 0)
                project(here, 1, KB, hhi, hlo, dense[1]).then_inc(block_done.sem, 1)

            layers(pe, pro, head, tail, nothing, merge, nothing, outs, True)

            pe.wait_ge(*last(x_ready))
            for n in range(NT):
                if n == 2:
                    pe.wait_ge(*last(sq_sum))
                    for t in range(NT):
                        ins = pe.matmul(m01[:, 2 * t:2 * t + 2], W[0][:, t * P:(t + 1) * P], ones[:, 0:2], start=True, stop=True)
                    ins.then_inc(ssq.sem, 1)
                if n >= 2:
                    pe.wait_ge(*once(fin_c, n - 1))
                for k in range(KB):
                    ins = pe.transpose(dense[n % 2][:, k * P:(k + 1) * P], xs[:, k, n * P:(n + 1) * P], ident)
                ins.then_inc(fin_t.sem, 1)

        @block.scalar
        def _(act):
            step = own["act"]
            LNEXP = "natural_log_exp_and_others"

            begin(act, *emptied, b_st, a_stored, c_stored, v_sh)
            act.dma_start(cst[:, 0:2 * P], consts[:, 0:2 * P]).then_inc(ident_in.sem, 16)
            act.preload_act_table_set(LNEXP)
            for n in range(NT):
                act.wait_ge(*once(x_c, n + 1))
                if n >= 2:
                    act.wait_ge(*early(sq_sum, n - 1))
                act.activation(tiles(W[5 + n % 2]), xs[:, :, n * P:(n + 1) * P], ACT.Square).then_inc(sq.sem, 1)
            act.wait_ge(*once(setup_c, 4))
            act.activation(prm[:, R_LB:R_LB + 8], small[:, 16:24], ACT.Exp).then_inc(setup_c.sem, 1)

            def pro(here, layer):
                n = [0]

                def mine():
                    n[0] += 1
                    act.wait_ge(*step.at(here, n[0]))

                act.preload_act_table_set(LNEXP)
                act.wait_ge(*ssq.at(here, 1))
                act.activation(W[3], m01, ACT.Ln, bias=EPS, scale=1.0 / D).then_inc(step.sem, 1)
                mine()
                act.activation(W[3], W[3], ACT.Exp, scale=-0.5).then_inc(rstd.sem, 1)
                act.wait_ge(*x_ready.at(here, 0))
                act.dma_start(x_d.rearrange("k p t -> p k t"), xs).then_inc(x_dst.sem, 16)
                act.dma_start(z2[:, 0:4 * P], dups).then_inc(dup_in.sem, 16)
                for k in range(KB):
                    act.wait_ge(*hn.at(here, k + 1))
                    act.activation(hhi[:, k, :], W[4 + k % 4], ACT.Copy).then_inc(h_hi.sem, 1)
                wait_lo(act, here, KB - 2)
                wait_lo(act, here, KB - 1)
                act.wait_ge(*if_copied.at(here, 1))
                act.dma_start(W[4][0:4, :], W[3][4:8, :]).then_inc(f_moved.sem, 16)
                act.wait_ge(*f_moved.at(here, 1))
                act.activation(W[5][0:4, :], W[4][0:4, :], ACT.Abs).then_inc(step.sem, 1)
                mine()
                act.activation(W[5][0:4, :], W[5][0:4, :], ACT.Exp, scale=-1.0).then_inc(step.sem, 1)
                mine()
                act.activation(W[5][0:4, :], W[5][0:4, :], ACT.Ln, bias=1.0).then_inc(r_abs.sem, 1)
                act.wait_ge(*block_done.at(here, 2))
                act.activation(W[0], dense[1], ACT.Copy).then_inc(k_copied.sem, 1)
                act.wait_ge(*k_copied.at(here, 1))
                act.sem_inc(emptied[1].sem, 1)
                act.wait_ge(*r_sums.at(here, 1))
                act.activation(W[6][0:4, :], W[6][0:4, :], ACT.Exp).then_inc(r_inter.sem, 1)
                act.activation(W[7][0:4, :], W[7][0:4, :], ACT.Exp, scale=-1.0).then_inc(step.sem, 1)
                mine()
                act.activation(W[5][0:4, :], W[5][0:4, :], ACT.Exp).then_inc(r_exp.sem, 1)
                act.wait_ge(*r_exp.at(here, 1))
                act.wait_ge(*r_dec.at(here, 1))
                for kind, src in enumerate((W[8], W[6], W[7], W[3], W[5])):
                    act.dma_start(row_d[kind], src[0:4, :]).then_inc(r_out.sem, 16)
                act.dma_start(dec_d.rearrange("o (h t) -> (o h) t", h=HEADS), small[0:4, 0:NT]).then_inc(r_out.sem, 16)
                act.wait_ge(*block_done.at(here, 3))
                act.activation(W[2], dense[0], ACT.Copy).then_inc(v_copied.sem, 1)
                act.wait_ge(*v_copied.at(here, 1))
                act.sem_inc(emptied[0].sem, 1)
                act.wait_ge(*v_t.at(here, 1))
                act.activation(vtok, dense[1], ACT.Copy).then_inc(v_tok.sem, 1)
                act.wait_ge(*v_tok.at(here, 1))
                act.sem_inc(emptied[1].sem, 1)
                act.dma_start(vsh[0:64, 0:7 * P], vtok[64:128, 0:7 * P]).then_inc(v_sh.sem, 16)
                act.dma_start(vsh[64:128, 0:7 * P], vtok[0:64, P:8 * P]).then_inc(v_sh.sem, 16)
                act.wait_ge(*r_out.at(here, 6))
                act.wait_ge(*x_dst.at(here, 1))
                for kind in (3, 4):
                    act.dma_start(W[5][0:32, (kind - 3) * P:(kind - 2) * P],
                                  row_d[kind].rearrange("h (t c) -> (h t) c", c=P)).then_inc(r_in.sem, 16)
                act.dma_start(dec, dec_d.partition_broadcast(P)).then_inc(r_in.sem, 16)

            def late_act(here, n):
                def mine():
                    n[0] += 1
                    act.wait_ge(*step.at(here, n[0]))

                def denominator():
                    act.wait_ge(*c_den.at(here, 1))
                    act.activation(W[3], m01, ACT.Abs).then_inc(c_ab.sem, 1)
                    act.wait_ge(*c_mx.at(here, 1))
                    act.activation(W[3], W[3], ACT.Ln).then_inc(step.sem, 1)
                    mine()
                    act.activation(W[3], W[3], ACT.Exp, scale=-1.0).then_inc(c_r.sem, 1)
                    act.wait_ge(*c_h.at(here, 1))
                    act.activation(W[4], W[8], ACT.Square).then_inc(c_sq.sem, 1)

                def norm():
                    act.wait_ge(*c_ss.at(here, 1))
                    act.activation(W[3], m01, ACT.Ln, bias=EPS, scale=1.0 / P).then_inc(step.sem, 1)
                    mine()
                    act.activation(W[3], W[3], ACT.Exp, scale=-0.5).then_inc(c_rs.sem, 1)

                def store(head_before):
                    act.wait_ge(*c_done.at(here, 1))
                    act.dma_start(u_d[2, head_before].rearrange("o p t -> p (o t)"), W[8]).then_inc(c_stored.sem, 16)

                return denominator, norm, store

            def tail(here, layer):
                n = [0]
                denominator, norm, store = late_act(here, n)
                first = ("branch", layer, 0)
                act.wait_ge(*a_stored.at(here, 0))
                act.wait_ge(*c_sc.at(here, 0))
                act.dma_start(us, u_d[0:1].rearrange("b k p t -> p (b k) t")).then_inc(u_in.sem, 16)
                act.preload_act_table_set(LNEXP)
                act.wait_ge(*u_in.at(first, 1))
                for k in U_ORDER[:3]:
                    act.activation(uhi[:, k, :], us[:, k, :], ACT.Copy).then_inc(u_hi.sem, 1)
                denominator()
                k = U_ORDER[3]
                act.activation(uhi[:, k, :], us[:, k, :], ACT.Copy).then_inc(u_hi.sem, 1)
                norm()
                store(slice(HEADS - 1, HEADS))
                assert n[0] == OWN["act"]["tail"], n

            def head(here, layer, i, g, late):
                n = [0]
                denominator, norm, store = late_act(here, n)

                def mine():
                    n[0] += 1
                    act.wait_ge(*step.at(here, n[0]))

                def empty(j, ev, dst, func, **kw):
                    act.wait_ge(*block_done.at(here, j + 1))
                    act.activation(dst, dense[j % 2], func, **kw).then_inc(ev.sem, 1)

                def emptied_by(ev, j):
                    act.wait_ge(*ev.at(here, 1))
                    act.sem_inc(emptied[j % 2].sem, 1)

                def decay(m):
                    act.wait_ge(*a_diff.at(here, m + 1))
                    act.activation(KQ[m], KQ[m], ACT.Exp).then_inc(a_e.sem, 1)

                def tap(j, ev, dst, col):
                    act.wait_ge(*block_done.at(here, j + 1))
                    act.wait_ge(*hp_done.at(here, 1))
                    act.activation(dst, dense[j % 2], ACT.Identity, bias=hp[:, col + 8:col + 9], scale=hp[:, col + 6:col + 7]).then_inc(ev.sem, 1)

                empty(0, b_q, bq, ACT.Copy)
                emptied_by(b_q, 0)
                act.wait_ge(*a_done.at(here, 0))
                empty(1, b_z, z0, ACT.Silu)
                emptied_by(b_z, 1)
                if late:
                    act.preload_act_table_set(LNEXP)
                    denominator()
                empty(2, a_sig, ak, ACT.Sigmoid)
                emptied_by(a_sig, 2)
                act.preload_act_table_set(LNEXP)
                if late:
                    norm()
                if late:
                    store(bass.ds(i - 1, 1))
                empty(3, a_q, aq, ACT.Silu)
                emptied_by(a_q, 3)
                act.preload_act_table_set(LNEXP)
                exps = n[0]
                for q in range(4):
                    act.wait_ge(*b_d.at(here, q + 1))
                    p = W[q // 2][:, (q % 2) * HALF:(q % 2 + 1) * HALF]
                    act.activation(p, p, ACT.Exp).then_inc(b_e.sem, 1)
                    act.activation(small[:, 32 + 4 * q:36 + 4 * q], small[:, 16 + 4 * q:20 + 4 * q], ACT.Exp).then_inc(step.sem, 1)
                    n[0] += 1
                assert exps == (2 if late else 0)
                tap(4, c_qc, cq, 0)
                def probs_copied(q):
                    act.wait_ge(*b_pt.at(here, q + 1))
                    act.activation(W[2 + q // 2][:, (q % 2) * HALF:(q % 2 + 1) * HALF], mb[q], ACT.Copy).then_inc(b_ptc.sem, 1)

                for q in range(3):
                    probs_copied(q)
                act.wait_ge(*a_f.at(here, 1))
                act.activation(z1, z1, ACT.Ln).then_inc(a_ln.sem, 1)
                decay(0)
                decay(1)
                probs_copied(3)
                empty(5, a_v, avt, ACT.Copy)
                emptied_by(a_v, 5)
                act.wait_ge(*b_done.at(here, 1))
                act.dma_start(u_d[1, bass.ds(i, 1)].rearrange("o p t -> p (o t)"), W[8]).then_inc(b_st.sem, 16)
                decay(2)
                decay(3)
                decay(4)
                act.activation(W[1], z2, ACT.Exp).then_inc(a_start.sem, 1)
                act.wait_ge(*a_vt.at(here, 1))
                act.activation(W[0], m01, ACT.Copy).then_inc(a_vtok.sem, 1)
                decay(5)
                tap(6, c_kc, ck, 1)
                decay(6)
                decay(7)
                act.wait_ge(*a_last.at(here, 1))
                act.activation(small[:, NT:2 * NT], small[:, 0:NT], ACT.Exp).then_inc(a_el.sem, 1)
                act.wait_ge(*a_lv.at(here, 1))
                empty(7, c_v, cvt, ACT.Copy)
                emptied_by(c_v, 7)
                act.wait_ge(*a_kt.at(here, 1))
                act.activation(W[7], m23, ACT.Copy).then_inc(a_ktc.sem, 1)
                act.wait_ge(*c_qt.at(here, 1))
                act.activation(cq, cq, ACT.Silu).then_inc(c_q.sem, 1)
                act.wait_ge(*emptied[0].at(here, 4))
                act.activation(ck, ck, ACT.Silu).then_inc(c_k.sem, 1)
                act.wait_ge(*b_done.at(here, 1))
                empty(8, a_z, z0, ACT.Silu)
                emptied_by(a_z, 8)
                act.wait_ge(*c_vt.at(here, 1))
                act.activation(W[5], m23, ACT.Copy).then_inc(c_vtok.sem, 1)
                empty(9, c_zo, z1, ACT.Sigmoid)
                emptied_by(c_zo, 9)
                act.wait_ge(*a_o.at(here, 1))
                act.dma_start(W[0], row_d[0, bass.ds(i, 1), :].partition_broadcast(P)).then_inc(c_in.sem, 16)
                act.dma_start(W[6], row_d[1, bass.ds(i, 1), :].partition_broadcast(P)).then_inc(c_in.sem, 16)
                act.dma_start(W[7], row_d[2, bass.ds(i, 1), :].partition_broadcast(P)).then_inc(c_in.sem, 16)
                act.activation(W[4], m23, ACT.Copy).then_inc(a_oc.sem, 1)
                act.wait_ge(*a_oc.at(here, 1))
                act.activation(W[2], W[4], ACT.Square).then_inc(a_sq.sem, 1)
                empty(10, c_zz, z2, ACT.Silu)
                emptied_by(c_zz, 10)
                act.preload_act_table_set(LNEXP)
                act.wait_ge(*c_dx.at(here, 1))
                act.activation(W[0], W[0], ACT.Exp).then_inc(c_dm.sem, 1)
                act.wait_ge(*a_ss.at(here, 1))
                act.activation(W[3], m23, ACT.Ln, bias=EPS, scale=1.0 / P).then_inc(step.sem, 1)
                mine()
                act.activation(W[3], W[3], ACT.Exp, scale=-0.5).then_inc(a_rs.sem, 1)
                act.wait_ge(*a_done.at(here, 1))
                act.dma_start(u_d[0, bass.ds(i, 1)].rearrange("o p t -> p (o t)"), W[8]).then_inc(a_stored.sem, 16)
                assert n[0] == OWN["act"]["head" if late else "head0"], n

            def branch(here, merging, b):
                act.wait_ge(*a_stored.at(here, 0))
                act.wait_ge(*b_st.at(here, 0))
                act.wait_ge(*c_stored.at(here, 0))
                act.wait_ge(*block_done.at(merging, 0))
                act.wait_ge(*u_lo.at(here, 0))
                act.dma_start(us, u_d[bass.ds(b, 1)].rearrange("b k p t -> p (b k) t")).then_inc(u_in.sem, 16)
                act.wait_ge(*u_in.at(here, 1))
                for k in U_ORDER:
                    act.activation(uhi[:, k, :], us[:, k, :], ACT.Copy).then_inc(u_hi.sem, 1)

            def merge(here, layer, b, d):
                for j in range(2):
                    act.wait_ge(*block_done.at(here, j + 1))
                    act.wait_ge(*br_taken.at(here, 0))
                    act.activation(ga[j], dense[j], ACT.Sigmoid, bias=bmg[:, bass.ds(layer * 24 + b * 8 + d * 2 + j, 1)]).then_inc(g_sig.sem, 1)
                    act.wait_ge(*g_sig.at(here, j + 1))
                    act.sem_inc(emptied[j].sem, 1)

            def join(here, layer):
                for k in range(KB):
                    act.wait_ge(*br_taken.at(("merge", layer, 8 + k // 2), k % 2 + 1))
                    act.activation(hhi[:, k, :], mg[:, k, :], ACT.Copy).then_inc(m_hi.sem, 1)

            def outs(here, layer, e):
                for j in range(2):
                    act.wait_ge(*emptied[j].at(here, 0))
                    act.dma_start(S(8 + j), x_d[bass.ds(e * 2 + j, 1)].rearrange("k p t -> p (k t)")).then_inc(xo_in[j].sem, 16)
                for j in range(2):
                    act.wait_ge(*x_ready.at(here, j + 1))
                    act.wait_ge(*sq_sum.at(here, j - 1))
                    act.activation(S(20 + j), slots[:, bass.ds(e * 2 + j, 1), :].rearrange("p o t -> p (o t)"), ACT.Square).then_inc(sq.sem, 1)

            layers(act, pro, head, tail, branch, merge, join, outs)

            act.preload_act_table_set(LNEXP)
            act.wait_ge(*last(ssq, 1))
            act.activation(small[:, 0:NT], m01[:, 0:2 * NT].rearrange("p (t o) -> p t o", o=2)[:, :, 0], ACT.Ln, bias=EPS, scale=1.0 / D).then_inc(fin.sem, 1)
            act.wait_ge(*once(fin, 1))
            act.activation(small[:, 0:NT], small[:, 0:NT], ACT.Exp, scale=-0.5).then_inc(rstd.sem, 1)
            act.wait_ge(*last(a_stored))
            act.wait_ge(*last(b_st))
            act.wait_ge(*last(c_stored))

        @block.vector
        def _(dve):
            step = own["dve"]

            def counted(here):
                n = [0]

                def link(ins):
                    n[0] += 1
                    ins.then_inc(step.sem, 1)
                    dve.wait_ge(*step.at(here, n[0]))
                return n, link

            def tally(phase, n):
                assert n[0] == OWN["dve"][phase], (phase, n)

            def told(here, ins, ev, k):
                ins.then_inc(ev.sem, 1)
                dve.wait_ge(*ev.at(here, k))

            begin(dve, b_done, a_done, c_done, br_taken, u_lo)
            def squares(n):
                dve.wait_ge(*early(sq, n + 1))
                dve.tensor_reduce(W[0][:, n * P:(n + 1) * P], W[5 + n % 2].rearrange("p (k c) -> p c k", c=P), AX, ALU.add).then_inc(sq_sum.sem, 1)

            def parameters():
                dve.wait_ge(*once(setup_t, 1))
                dve.tensor_copy(prm, m23[:, 0:R_END]).then_inc(setup_c.sem, 1)
                dve.tensor_copy(bmg, m23[:, 128:128 + DEPTH * 24]).then_inc(setup_c.sem, 1)
                dve.wait_ge(*once(setup_c, 2))
                dve.tensor_tensor(small[:, 0:4], prm[:, R_LB:R_LB + 4], prm[:, R_LB + 4:R_LB + 8], ALU.max).then_inc(setup_c.sem, 1)
                dve.wait_ge(*once(setup_c, 3))
                lb3 = prm[:, R_LB:R_LB + 8].rearrange("p (l h) -> p l h", l=2)
                mx3 = small[:, 0:4].unsqueeze(1).to_broadcast([P, 2, 4])
                dve.tensor_tensor(small[:, 16:24].rearrange("p (l h) -> p l h", l=2), lb3, mx3, ALU.subtract).then_inc(setup_c.sem, 1)
                dve.wait_ge(*once(setup_c, 5))
                e0, e1 = prm[:, R_LB:R_LB + 4], prm[:, R_LB + 4:R_LB + 8]
                k = [5]

                def then(ins):
                    k[0] += 1
                    ins.then_inc(setup_c.sem, 1)
                    dve.wait_ge(*once(setup_c, k[0]))
                then(dve.tensor_tensor(small[:, 0:4], e0, e1, ALU.add))
                then(dve.reciprocal(small[:, 4:8], small[:, 0:4]))
                then(dve.tensor_tensor(small[:, 8:12], e0, small[:, 4:8], ALU.mult))
                then(dve.tensor_tensor(small[:, 12:16], e1, small[:, 4:8], ALU.mult))
                then(dve.tensor_tensor(small[:, 0:4], small[:, 8:12], small[:, 12:16], ALU.add))
                then(dve.tensor_tensor(e0, small[:, 8:12], small[:, 8:12], ALU.subtract))
                then(dve.tensor_tensor(e1, small[:, 0:4], small[:, 8:12], ALU.subtract))
                for h in range(2):
                    r = slice(h * CHUNK, (h + 1) * CHUNK)
                    then(dve.tensor_copy(sinks[r, :], sinks_all[r, :].rearrange("p (c h) -> p c h", h=2)[:, :, h]))

            for n in range(NT):
                dve.wait_ge(*once(x_t, n + 1))
                dve.tensor_copy(xs[:, :, n * P:(n + 1) * P], dense[n % 2].rearrange("p (k c) -> p k c", c=P)).then_inc(x_c.sem, 1)
                if n:
                    squares(n - 1)
            squares(NT - 1)
            parameters()
            dve.wait_ge(*once(x_c, NT))
            dve.sem_inc(x_ready.sem, 1)
            dve.wait_ge(*once(table_in, 1))

            def pro(here, layer):
                n, link = counted(here)
                plain(dve)
                link(dve.tensor_copy(ng, prm[:, bass.ds(layer * KB + R_NG, KB)]))
                dve.wait_ge(*rstd.at(here, 1))
                for k in range(KB):
                    if k >= 4:
                        wait_lo(dve, here, k - 4)
                    ins = dve.scalar_tensor_tensor(W[4 + k % 4], xs[:, k, :], ng[:, k:k + 1], W[3], ALU.mult, ALU.mult)
                    told(here, ins, hn, k + 1)
                    if k % 2:
                        lo(here, k - 1)
                dve.wait_ge(*block_done.at(here, 1))
                told(here, dve.tensor_scalar(W[3][0:8, :], dense[0][0:8, :], gb[0:8, bass.ds(layer, 1)], None, ALU.add), if_copied, 1)
                dve.sem_inc(emptied[0].sem, 1)
                dve.wait_ge(*f_moved.at(here, 1))
                f, lf, cum, m, a, ig, wend = W[4][0:4, :], W[6][0:4, :], W[1][0:4, :], W[7][0:4, :], W[8][0:4, :], W[3][0:4, :], W[5][0:4, :]
                link(dve.tensor_scalar(lf, f, 0.0, None, ALU.min))
                dve.wait_ge(*r_abs.at(here, 1))
                link(dve.tensor_tensor(lf, lf, wend, ALU.subtract))
                link(dve.tensor_tensor_scan(m, lf, ig, 0.0, ALU.add, ALU.max))
                for t in range(NT):
                    c = slice(t * P, (t + 1) * P)
                    link(dve.tensor_tensor_scan(cum[:, c], ones[0:4, :], lf[:, c], 0.0, ALU.mult, ALU.add))
                link(dve.tensor_tensor(a, cum, m, ALU.subtract))
                link(dve.tensor_tensor(ig, ig, cum, ALU.subtract))
                link(dve.tensor_tensor(tiles(wend), tiles(ig), tiles(a)[:, :, P - 1:P].to_broadcast([4, NT, P]), ALU.add))
                link(dve.tensor_copy(lf[:, 0:P], a[:, 0:P]))
                told(here, dve.tensor_tensor(tiles(lf)[:, 1:NT, :], tiles(a)[:, 1:NT, :],
                                             tiles(m)[:, 0:NT - 1, P - 1:P].to_broadcast([4, NT - 1, P]), ALU.add), r_sums, 1)
                dve.wait_ge(*r_inter.at(here, 1))
                told(here, dve.tensor_copy(small[0:4, 0:NT], tiles(lf)[:, :, P - 1]), r_dec, 1)
                for g in range(2):
                    dve.wait_ge(*k_rot.at(here, 2 * g + 1))
                    told(here, dve.tensor_tensor(kd[g], m01, cos, ALU.mult), k_cos, 2 * g + 1)
                    dve.wait_ge(*k_rot.at(here, 2 * g + 2))
                    told(here, dve.tensor_tensor(z1, m23, sin, ALU.mult), k_cos, 2 * g + 2)
                    told(here, dve.tensor_tensor(kd[g], kd[g], z1, ALU.add), kd_done, g + 1)
                tally("pro", n)

            def lo(here, k):
                dve.wait_ge(*h_hi.at(here, k + 1))
                dve.tensor_tensor(hlo[:, k, :], W[4 + k % 4], hhi[:, k, :].bitcast(F32), ALU.subtract).then_inc(h_lo[0].sem, 1)

            def late_dve(here, former, link):
                def states():
                    dve.wait_ge(*c_u.at(here, 1))
                    link(dve.memset(nst[:, 0:1], 0.0))
                    plain(dve)
                    link(dve.tensor_copy(small[:, 0:NT], dec[:, former * NT:(former + 1) * NT] if isinstance(former, int) else dec[:, bass.ds(former * NT, NT)]))
                    for t in range(1, NT):
                        c, before = slice(t * P, (t + 1) * P), slice((t - 1) * P, t * P)
                        if t == 1:
                            link(dve.tensor_copy(nst[:, 1:2], m01[:, 0:1]))
                            ins = dve.tensor_copy(cst_v[:, c], m23[:, before])
                        else:
                            link(dve.scalar_tensor_tensor(nst[:, t:t + 1], nst[:, t - 1:t], small[:, t - 1:t], m01[:, 2 * t - 2:2 * t - 1], ALU.mult, ALU.add))
                            ins = dve.scalar_tensor_tensor(cst_v[:, c], cst_v[:, before], small[:, t - 1:t], m23[:, before], ALU.mult, ALU.add)
                        if t == NT - 1:
                            told(here, ins, c_st, 1)
                        else:
                            link(ins)
                    link(dve.tensor_tensor(tiles(W[2]), tiles(W[6]), nst.unsqueeze(2).to_broadcast([P, NT, P]), ALU.mult))
                    told(here, dve.tensor_tensor(W[2], W[2], W[0], ALU.add), c_t, 1)

                def denominator():
                    dve.wait_ge(*c_ab.at(here, 1))
                    told(here, dve.tensor_tensor(W[3], W[3], W[7], ALU.max), c_mx, 1)
                    dve.wait_ge(*c_r.at(here, 1))
                    dve.wait_ge(*c_o.at(here, 1))
                    dve.wait_ge(*a_stored.at(here, 0))
                    told(here, dve.tensor_tensor(W[8], m23, W[3], ALU.mult), c_h, 1)

                def finish():
                    dve.wait_ge(*c_rs.at(here, 1))
                    link(dve.scalar_tensor_tensor(W[8], W[8], hp[:, 15:16], W[3], ALU.mult, ALU.mult))
                    link(dve.tensor_tensor(W[8], W[8], z1, ALU.mult))
                    told(here, dve.tensor_tensor(W[8], W[8], z2, ALU.mult), c_done, 1)

                return states, denominator, finish

            def output_lo(here, n):
                k = U_ORDER[n]
                dve.wait_ge(*u_hi.at(here, n + 1))
                dve.tensor_tensor(ulo[:, k, :], us[:, k, :], uhi[:, k, :].bitcast(F32), ALU.subtract).then_inc(u_lo.sem, 1)

            def tail(here, layer):
                n, link = counted(here)
                states, denominator, finish = late_dve(here, HEADS - 1, link)
                first = ("branch", layer, 0)
                link(dve.tensor_copy(hp[:, 15:16], hp[:, 13:14]))
                states()
                for k in range(3):
                    output_lo(first, k)
                denominator()
                output_lo(first, 3)
                finish()
                tally("tail", n)

            def head(here, layer, i, g, late):
                n, link = counted(here)
                states, denominator, finish = late_dve(here, i - 1, link)
                if late:
                    link(dve.tensor_copy(hp[:, 15:16], hp[:, 13:14]))
                for w in range(4):
                    plain(dve)
                    link(dve.tensor_copy(hp[:, 2 * w:2 * w + 2], prm[:, bass.ds(layer * 32 + i + w * 8, 5)][:, 0:5:4]))
                plain(dve)
                link(dve.tensor_copy(hp[:, 8:10], prm[:, bass.ds(layer * 8 + i + R_CB, 5)][:, 0:5:4]))
                plain(dve)
                link(dve.tensor_copy(hp[:, 10:11], prm[:, bass.ds(layer * 4 + i + R_LB, 1)]))
                plain(dve)
                link(dve.tensor_copy(hp[:, 12:13], prm[:, bass.ds(layer + R_AG, 1)]))
                plain(dve)
                link(dve.tensor_copy(hp[:, 13:14], prm[:, bass.ds(layer * 4 + i + R_CG, 1)]))
                plain(dve)
                link(dve.tensor_copy(hp[:, 14:15], sinks[:, bass.ds(layer * 4 + i, 1)]))
                told(here, dve.tensor_scalar(hp[:, 11:12], hp[:, 10:11], -1.0, 1.0, ALU.mult, ALU.add), hp_done, 1)
                if late:
                    states()
                    denominator()
                else:
                    dve.wait_ge(*r_t.at(here, 1))
                    link(dve.tensor_copy(bcol, mb[2][:, 0:32]))
                    told(here, dve.tensor_copy(wcol, mb[2][:, 32:64]), r_col, 1)
                plain(dve)
                link(dve.tensor_copy(W[6], slots[:, bass.ds(g + 19, 1), :].rearrange("p o t -> p (o t)")))
                dve.wait_ge(*b_rope.at(here, 1))
                link(dve.tensor_tensor(W[7], m23, sin, ALU.mult))
                link(dve.tensor_tensor(bq, bq, cos, ALU.mult))
                told(here, dve.tensor_tensor(bq, bq, W[7], ALU.add), b_qr, 1)
                if late:
                    finish()
                dve.wait_ge(*v_sh.at(("head", layer, 0), 0))
                for src, dst, m in ((vtok, W[4], NT), (vsh, W[5], NT - 1)):
                    for h in range(2):
                        v = src.rearrange("p (t g c) -> p g t c", g=2, c=CHUNK)[:, bass.ds(g, 1), 0:m, :].rearrange("p o t c -> p (o t) c")
                        plain(dve)
                        link(dve.tensor_copy(dst.rearrange("p (t g c) -> p t g c", g=2, c=CHUNK)[:, 0:m, h, :], v))
                sc_mx, sc_d, sc_e, sc_s, sc_r = (small[:, 16 * m:16 * m + 16] for m in range(5))
                for q in range(4):
                    c4 = slice(4 * q, 4 * q + 4)
                    dve.wait_ge(*b_s.at(here, q + 1))
                    if q == 0:
                        link(dve.memset(mb[0][:, CHUNK:P], NEG))
                    s3 = mb[q].rearrange("p (c k) -> p c k", k=P)
                    p3 = tiles(W[q // 2])[:, (q % 2) * 4:(q % 2) * 4 + 4, :]
                    link(dve.tensor_reduce(sc_mx[:, c4], s3, AX, ALU.max))
                    link(dve.tensor_scalar(sc_mx[:, c4], sc_mx[:, c4], SCALE_B, hp[:, 14:15], ALU.mult, ALU.max))
                    link(dve.tensor_scalar(sc_d[:, c4], sc_mx[:, c4], -1.0, hp[:, 14:15], ALU.mult, ALU.add))
                    told(here, dve.scalar_tensor_tensor(p3, s3, SCALE_B, sc_mx[:, c4].unsqueeze(2).to_broadcast([P, 4, P]), ALU.mult, ALU.subtract), b_d, q + 1)
                for q in range(4):
                    c4 = slice(4 * q, 4 * q + 4)
                    p3 = tiles(W[q // 2])[:, (q % 2) * 4:(q % 2) * 4 + 4, :]
                    dve.wait_ge(*b_e.at(here, q + 1))
                    link(dve.tensor_reduce(sc_s[:, c4], p3, AX, ALU.add))
                    dve.wait_ge(*own["act"].at(here, (2 if late else 0) + q + 1))
                    link(dve.tensor_tensor(sc_s[:, c4], sc_s[:, c4], sc_e[:, c4], ALU.add))
                    link(dve.reciprocal(sc_r[:, c4], sc_s[:, c4]))
                    told(here, dve.tensor_tensor(p3, p3, sc_r[:, c4].unsqueeze(2).to_broadcast([P, 4, P]), ALU.mult), b_p, q + 1)

                dve.wait_ge(*a_sig.at(here, 1))
                link(dve.tensor_scalar(ak, ak, hp[:, 11:12], hp[:, 10:11], ALU.mult, ALU.add))
                told(here, dve.tensor_scalar(z1, ak, TINY, None, ALU.max), a_f, 1)
                told(here, dve.tensor_scalar(ak, ak, -1.0, 1.0, ALU.mult, ALU.add), a_k, 1)
                def taps(j, ev, dst, col, out_ev):
                    dve.wait_ge(*ev.at(here, 1))
                    src = dense[j % 2]
                    for w in (2, 1, 0):
                        d = 3 - w
                        ins = dve.scalar_tensor_tensor(dst[:, d:T], src[:, 0:T - d], hp[:, 2 * w + col:2 * w + col + 1], dst[:, d:T], ALU.mult, ALU.add)
                        if w == 0 and out_ev is not None:
                            told(here, ins, out_ev, 1)
                        elif w == 0:
                            ins.then_inc(emptied[j % 2].sem, 1)
                            dve.wait_ge(*emptied[j % 2].at(here, j // 2 + 1))
                        else:
                            link(ins)
                    if out_ev is not None:
                        dve.sem_inc(emptied[j % 2].sem, 1)

                taps(4, c_qc, cq, 0, c_qt)
                cum = z2
                dve.wait_ge(*a_ln.at(here, 1))
                for t in range(NT):
                    c = slice(t * P, (t + 1) * P)
                    ins = dve.tensor_tensor_scan(z2[:, c], ones, z1[:, c], 0.0, ALU.mult, ALU.add)
                    if t == NT - 1:
                        told(here, ins, a_cum, 1)
                    else:
                        link(ins)

                def exponents(m):
                    kq = KQ[m]
                    if m >= 6:
                        dve.wait_ge(*a_lv.at(here, m - 3))
                    if m == 7:
                        told(here, dve.tensor_tensor(tiles(kq), tiles(cum)[:, :, P - 1:P].to_broadcast([P, NT, P]), tiles(cum), ALU.subtract), a_diff, 8)
                        return
                    h = 64 >> m
                    c3, k3 = (v.rearrange("p (b e) -> p b e", e=2 * h) for v in (cum, kq))
                    ref = c3[:, :, h - 1:h].to_broadcast([P, T // (2 * h), h])
                    link(dve.tensor_tensor(k3[:, :, h:2 * h], c3[:, :, h:2 * h], ref, ALU.subtract))
                    told(here, dve.tensor_tensor(k3[:, :, 0:h], ref, c3[:, :, 0:h], ALU.subtract), a_diff, m + 1)

                def decayed(m):
                    kq = KQ[m]
                    dve.wait_ge(*a_e.at(here, m + 1))
                    if m == 7:
                        told(here, dve.tensor_tensor(kq, kq, ak, ALU.mult), a_kq, 8)
                        return
                    h = 64 >> m
                    k3, q3, f3 = (v.rearrange("p (b e) -> p b e", e=2 * h) for v in (kq, aq, ak))
                    link(dve.scalar_tensor_tensor(k3[:, :, h:2 * h], q3[:, :, h:2 * h], SCALE, k3[:, :, h:2 * h], ALU.mult, ALU.mult))
                    told(here, dve.tensor_tensor(k3[:, :, 0:h], k3[:, :, 0:h], f3[:, :, 0:h], ALU.mult), a_kq, m + 1)

                def taken(m):
                    h = 64 >> m
                    dve.wait_ge(*a_lv.at(here, m + 1))
                    o = tiles(W[6]).rearrange("p t (b e) -> p t b e", e=2 * h)[:, :, :, h:2 * h]
                    mask = cst[:, C_LVL + 64 * m:C_LVL + 64 * m + 64].bitcast(I32).rearrange("p (b r) -> p b r", r=h)
                    mask = mask.unsqueeze(1).to_broadcast([P, NT, 64 // h, h])
                    data = mb[LEVEL_BANK[m]].rearrange("p (t b r) -> p t b r", t=NT, r=h)
                    plain(dve)
                    told(here, dve.copy_predicated(o, mask, data), a_pr, m + 1)

                exponents(0)
                exponents(1)
                dve.wait_ge(*a_q.at(here, 1))
                decayed(0)
                decayed(1)
                dve.wait_ge(*b_z.at(here, 1))
                dve.wait_ge(*c_stored.at(here, 1 if late else 0))
                for q in range(4):
                    dve.wait_ge(*b_o.at(here, q + 1))
                    for h in range(2):
                        r = slice(h * CHUNK, (h + 1) * CHUNK)
                        o3 = mb[q][r, :].rearrange("p (c k) -> p c k", k=P)[:, :, h * CHUNK:(h + 1) * CHUNK]
                        cc = slice(q * 256, (q + 1) * 256)
                        ins = dve.tensor_tensor(W[8][r, cc].rearrange("p (c k) -> p c k", k=CHUNK), o3,
                                                z0[r, cc].rearrange("p (c k) -> p c k", k=CHUNK), ALU.mult)
                        if (q, h) == (3, 1):
                            told(here, ins, b_done, 1)
                        else:
                            link(ins)
                exponents(2)
                exponents(3)
                decayed(2)
                exponents(4)
                decayed(3)
                decayed(4)
                exponents(5)
                dve.wait_ge(*a_dg.at(here, 1))
                for h in range(2):
                    idb = ident.unsqueeze(1).to_broadcast([P, 4, P])
                    told(here, dve.scalar_tensor_tensor(tiles(W[6])[:, 4 * h:4 * h + 4, :], tiles(m23)[:, 4 * h:4 * h + 4, :], SCALE, idb, ALU.mult, ALU.mult), a_sa, h + 1)
                taken(0)
                taken(1)
                decayed(5)
                exponents(6)
                taken(2)
                taps(6, c_kc, ck, 1, None)
                decayed(6)
                exponents(7)
                taken(3)
                decayed(7)
                dve.wait_ge(*a_start.at(here, 1))
                told(here, dve.scalar_tensor_tensor(W[1], aq, SCALE, W[1], ALU.mult, ALU.mult), a_kq, 9)
                told(here, dve.tensor_copy(small[:, 0:NT], tiles(cum)[:, :, P - 1]), a_last, 1)
                taken(4)
                taken(5)
                taken(6)
                dve.wait_ge(*a_vt.at(here, 1))
                dve.wait_ge(*a_el.at(here, 1))
                dve.wait_ge(*a_u.at(here, 1))
                for t in range(1, NT):
                    c, before = slice(t * P, (t + 1) * P), slice((t - 1) * P, t * P)
                    if t == 1:
                        ins = dve.tensor_copy(ast[:, c], m01[:, before])
                    else:
                        ins = dve.scalar_tensor_tensor(ast[:, c], ast[:, before], small[:, 8 + t - 1:8 + t], m01[:, before], ALU.mult, ALU.add)
                    if t == NT - 1:
                        told(here, ins, a_st, 1)
                    else:
                        link(ins)
                dve.wait_ge(*c_kt.at(here, 1))
                dve.wait_ge(*a_o.at(here, 1))
                for h in range(2):
                    wb = wcol[:, bass.ds(i * NT + 4 * h, 4)].unsqueeze(2).to_broadcast([P, 4, P])
                    told(here, dve.tensor_tensor(tiles(W[1])[:, 4 * h:4 * h + 4, :], tiles(m01)[:, 4 * h:4 * h + 4, :], wb, ALU.mult), c_kw, h + 1)
                dve.wait_ge(*c_in.at(here, 3))
                d3 = tiles(W[0])
                link(dve.tensor_tensor(d3, d3, negm.unsqueeze(1).to_broadcast([P, NT, P]), ALU.add))
                told(here, dve.tensor_tensor(d3, d3, bcol[:, bass.ds(i * NT, NT)].unsqueeze(2).to_broadcast([P, NT, P]), ALU.add), c_dx, 1)
                dve.wait_ge(*c_q.at(here, 1))
                told(here, dve.scalar_tensor_tensor(W[6], cq, SCALE, W[6], ALU.mult, ALU.mult), c_qp, 1)
                dve.wait_ge(*c_dm.at(here, 1))
                dve.wait_ge(*c_s.at(here, 1))
                for h in range(2):
                    t = slice(h * HALF, (h + 1) * HALF)
                    told(here, dve.scalar_tensor_tensor(W[0][:, t], m01[:, t], SCALE, W[0][:, t], ALU.mult, ALU.mult), c_sc, h + 1)
                dve.wait_ge(*a_rs.at(here, 1))
                dve.wait_ge(*a_z.at(here, 1))
                dve.wait_ge(*b_st.at(here, 1))
                link(dve.scalar_tensor_tensor(W[8], W[4], hp[:, 12:13], W[3], ALU.mult, ALU.mult))
                told(here, dve.tensor_tensor(W[8], W[8], z0, ALU.mult), a_done, 1)
                tally("head" if late else "head0", n)

            def branch(here, merging, b):
                for n in range(4):
                    output_lo(here, n)

            def merge(here, layer, b, d):
                n, link = counted(here)
                for j in range(2):
                    dve.wait_ge(*g_sig.at(here, j + 1))
                    if j == 0:
                        dve.wait_ge(*br_done.at(here, 1))
                    else:
                        dve.wait_ge(*block_done.at(here, 3))
                    dst = slots[:, bass.ds(d * 2 + (12 + j), 1), :].rearrange("p o t -> p (o t)")
                    if isinstance(b, int):
                        dve.wait_ge(*c_stored.at(here, 0))
                        n[0] += 1
                        dve.sem_inc(step.sem, 1)
                        told(here, dve.tensor_tensor(dst, ga[j], (m01, m23)[j], ALU.mult), br_taken, j + 1)
                    else:
                        link(dve.tensor_tensor(gt, ga[j], (m01, m23)[j], ALU.mult))
                        told(here, dve.tensor_tensor(dst, dst, gt, ALU.add), br_taken, j + 1)
                tally("merge", n)

            def join(here, layer):
                for k in range(KB):
                    dve.wait_ge(*m_hi.at(here, k + 1))
                    dve.tensor_tensor(hlo[:, k, :], mg[:, k, :], hhi[:, k, :].bitcast(F32), ALU.subtract).then_inc(m_lo.sem, 1)

                told(here, dve.memset(W[0], 0.0), sum_cleared, 1)

            def outs(here, layer, e):
                for j in range(2):
                    dve.wait_ge(*block_done.at(here, j + 1))
                    dve.wait_ge(*xo_in[j].at(here, 1))
                    dst = slots[:, bass.ds(e * 2 + j, 1), :].rearrange("p o t -> p (o t)")
                    told(here, dve.tensor_tensor(dst, dense[j], S(8 + j), ALU.add), x_ready, j + 1)
                    dve.sem_inc(emptied[j].sem, 1)
                    dve.wait_ge(*sq.at(here, j + 1))
                    told(here, dve.tensor_tensor(W[0], W[0], S(20 + j), ALU.add), sq_sum, j + 1)

            layers(dve, pro, head, tail, branch, merge, join, outs, True)

            dve.wait_ge(*last(rstd, 1))
            dve.wait_ge(*once(fin_g, 1))
            for n in range(NT):
                dve.wait_ge(*once(fin_t, n + 1))
                if n >= 4:
                    dve.wait_ge(*once(y_out[n % 4], n // 4))
                dve.scalar_tensor_tensor(W[4 + n % 4], dense[n % 2], small[:, n:n + 1], mg[:, 0, :], ALU.mult, ALU.mult).then_inc(fin_c.sem, 1)


_INS = ["x", "norm_g", "w_in", "conv_w", "conv_b", "hgrn_lb", "hgrn_norm_g", "attn_sinks", "mlstm_gate_b",
        "mlstm_norm_g", "w_mg", "b_mg", "w_br", "w_out", "final_g"]


def kernel(**inputs):
    import concourse.bacc as bacc
    from concourse.bass_utils import run_bass_kernel_spmd

    nc = bacc.Bacc("TRN2", target_bir_lowering=False, num_devices=1)
    table, dups = constants()
    arrays = {f"in_{n}": np.ascontiguousarray(inputs[n]) for n in _INS} | {"in_consts": table, "in_dups": dups}
    args = {n[3:]: nc.dram_tensor(n, a.shape, mybir.dt.from_np(a.dtype), kind="ExternalInput").ap() for n, a in arrays.items()}
    args["out"] = nc.dram_tensor("out_0", (1, T, D), F32, kind="ExternalOutput").ap()
    build(nc, **args)
    return run_bass_kernel_spmd(nc, [arrays], core_ids=[0]).results[0]["out_0"]
```
